# Optimizing a Trainium2 kernel written in Bass

```python
import math
import jax
import jax.numpy as jnp
from jax import lax
import numpy as np

D_MODEL = 1024
BATCH = 1
SEQ = 512
DEPTH = 1

DIFF_HEADS = 4
DIFF_HD = 64
DIFF_VD = 2 * DIFF_HD
DIL_PATTERNS = ((128, 1), (512, 4), (2048, 16))
N_DIL_GROUPS = len(DIL_PATTERNS)
DIL_HEADS = 4
DIL_HD = 64
REL_BUCKETS = 32
REL_MAX_DIST = 2048
N_ATTN_HEADS = DIFF_HEADS + N_DIL_GROUPS * DIL_HEADS
PEER_HEADS = 8
PEER_NKEYS = 128
PEER_TOPK = 16
PEER_DKEY = 128
N_EXPERTS = PEER_NKEYS * PEER_NKEYS
Q_BLOCK = 128
TOKEN_BLOCK = 128
ALPHA = (2.0 * DEPTH) ** 0.25
BETA = (8.0 * DEPTH) ** -0.25
LN_EPS = 1e-5
SUBLN_EPS = 1e-5

DIFF_QK_W = DIFF_HEADS * 2 * DIFF_HD
DIFF_V_W = DIFF_HEADS * DIFF_VD
DIL_W = N_DIL_GROUPS * DIL_HEADS * DIL_HD
DIL_OUT_W = DIL_HEADS * DIL_HD
OFF_DQ = 0
OFF_DK = OFF_DQ + DIFF_QK_W
OFF_DV = OFF_DK + DIFF_QK_W
OFF_LQ = OFF_DV + DIFF_V_W
OFF_LK = OFF_LQ + DIL_W
OFF_LV = OFF_LK + DIL_W
OFF_GA = OFF_LV + DIL_W
OFF_GB = OFF_GA + D_MODEL
IN_COLS = OFF_GB + D_MODEL

kernel_name = 'hybrid_diffattn_dilated_peer_deepnorm'

def layer_norm(x, g, b):
    xf = x.astype(jnp.float32)
    mu = jnp.mean(xf, axis=-1, keepdims=True)
    var = jnp.mean(jnp.square(xf - mu), axis=-1, keepdims=True)
    return ((xf - mu) * lax.rsqrt(var + LN_EPS) * g + b).astype(x.dtype)

def rel_bucket(dist):
    n = jnp.maximum(dist, 0)
    max_exact = REL_BUCKETS // 2
    nf = jnp.maximum(n, 1).astype(jnp.float32)
    large = max_exact + (jnp.log(nf / max_exact) / math.log(REL_MAX_DIST / max_exact)
                         * (REL_BUCKETS - max_exact)).astype(jnp.int32)
    large = jnp.minimum(large, REL_BUCKETS - 1)
    return jnp.where(n < max_exact, n, large)

def diff_attention(q, k, v, lam, lam_init, bias_dist, subln_g):
    B, S, H = q.shape[0], q.shape[1], q.shape[2]
    nb = S // Q_BLOCK
    qb = jnp.moveaxis(q.reshape(B, nb, Q_BLOCK, H, 2, DIFF_HD), 1, 0)
    kpos = jnp.arange(S)
    scale = DIFF_HD ** -0.5

    def block(args):
        qi, i = args
        qpos = i * Q_BLOCK + jnp.arange(Q_BLOCK)
        dist = qpos[:, None] - kpos[None, :]
        bias = jnp.moveaxis(jnp.take(bias_dist, jnp.clip(dist, 0, S - 1), axis=0), -1, 0)
        logits = jnp.einsum('bqhcd,bkhcd->bchqk', qi, k).astype(jnp.float32) * scale
        logits = logits + bias.astype(jnp.float32)[None, None]
        logits = jnp.where(dist >= 0, logits, -jnp.inf)
        p = jax.nn.softmax(logits, axis=-1)
        attn = p[:, 0] - lam * p[:, 1]
        return jnp.einsum('bhqk,bkhe->bqhe', attn.astype(v.dtype), v)

    out = lax.map(block, (qb, jnp.arange(nb)))
    out = jnp.moveaxis(out, 0, 1).reshape(B, S, H, DIFF_VD).astype(jnp.float32)
    out = out * lax.rsqrt(jnp.mean(jnp.square(out), axis=-1, keepdims=True) + SUBLN_EPS)
    out = out * subln_g * (1.0 - lam_init)
    return out.reshape(B, S, H * DIFF_VD)

def dilated_group(q, k, v, window, dilation, bias_h):
    B, S, H, dh = q.shape
    n_off = window // dilation + 1
    offs = jnp.arange(n_off) * dilation
    bias = jnp.take(bias_h, rel_bucket(offs), axis=0).astype(jnp.float32)
    kp = jnp.pad(k, ((0, 0), (window, 0), (0, 0), (0, 0)))
    vp = jnp.pad(v, ((0, 0), (window, 0), (0, 0), (0, 0)))
    nb = S // Q_BLOCK
    qb = jnp.moveaxis(q.reshape(B, nb, Q_BLOCK, H, dh), 1, 0)
    scale = dh ** -0.5

    def block(args):
        qi, i = args
        qpos = i * Q_BLOCK + jnp.arange(Q_BLOCK)
        kpos = qpos[:, None] - offs[None, :]
        kg = jnp.take(kp, kpos + window, axis=1)
        vg = jnp.take(vp, kpos + window, axis=1)
        logits = jnp.einsum('bqhd,bqjhd->bhqj', qi, kg).astype(jnp.float32) * scale
        logits = logits + bias.T[None, :, None, :]
        logits = jnp.where(kpos >= 0, logits, -jnp.inf)
        lse = jax.nn.logsumexp(logits, axis=-1)
        p = jnp.exp(logits - lse[..., None])
        o = jnp.einsum('bhqj,bqjhd->bqhd', p, vg.astype(jnp.float32))
        return o, lse

    o, lse = lax.map(block, (qb, jnp.arange(nb)))
    o = jnp.moveaxis(o, 0, 1).reshape(B, S, H, dh)
    lse = jnp.transpose(lse, (1, 0, 3, 2)).reshape(B, S, H)
    return o, lse

def dilated_attention(q, k, v, rel_bias_dil):
    B, S = q.shape[0], q.shape[1]
    outs, lses = [], []
    for g, (window, dilation) in enumerate(DIL_PATTERNS):
        o, lse = dilated_group(q[:, :, g], k[:, :, g], v[:, :, g], window, dilation,
                               rel_bias_dil[:, g * DIL_HEADS:(g + 1) * DIL_HEADS])
        outs.append(o)
        lses.append(lse)
    o_all = jnp.stack(outs, axis=2)
    w = jax.nn.softmax(jnp.stack(lses, axis=2), axis=2)
    out = jnp.sum(w[..., None] * o_all, axis=2)
    return out.reshape(B, S, DIL_OUT_W)

def peer(x, w_q, sub_keys, u, v):
    B, S, D = x.shape
    T = B * S
    xt = x.reshape(T // TOKEN_BLOCK, TOKEN_BLOCK, D)

    def block(xb):
        qb = (xb @ w_q).reshape(TOKEN_BLOCK, PEER_HEADS, 2, PEER_DKEY)
        s = jnp.einsum('thcd,hcnd->thcn', qb, sub_keys).astype(jnp.float32)
        s_top, i_top = lax.top_k(s, PEER_TOPK)
        cand = s_top[:, :, 0, :, None] + s_top[:, :, 1, None, :]
        cand_idx = i_top[:, :, 0, :, None] * PEER_NKEYS + i_top[:, :, 1, None, :]
        cand = cand.reshape(TOKEN_BLOCK, PEER_HEADS, PEER_TOPK * PEER_TOPK)
        cand_idx = cand_idx.reshape(TOKEN_BLOCK, PEER_HEADS, PEER_TOPK * PEER_TOPK)
        best, pos = lax.top_k(cand, PEER_TOPK)
        eidx = jnp.take_along_axis(cand_idx, pos, axis=-1)
        g = jax.nn.softmax(best, axis=-1)
        ug = jnp.take(u, eidx, axis=0)
        vg = jnp.take(v, eidx, axis=0)
        h = jax.nn.gelu(jnp.einsum('td,thkd->thk', xb, ug).astype(jnp.float32), approximate=False)
        return jnp.einsum('thk,thkd->td', (g * h).astype(x.dtype), vg)

    return lax.map(block, xt).reshape(B, S, D)

def setup_inputs(seed: int = 0) -> dict:
    key = jax.random.key(seed)
    ks = jax.random.split(key, 16)
    f32 = jnp.float32
    L = DEPTH
    x = jax.random.normal(ks[0], (BATCH, SEQ, D_MODEL), f32)
    col_scale = jnp.ones((IN_COLS,), f32).at[OFF_DV:OFF_LQ].set(BETA).at[OFF_LV:OFF_GA].set(BETA)
    w_in = jax.random.normal(ks[1], (L, D_MODEL, IN_COLS), f32) * D_MODEL ** -0.5 * col_scale
    diff_lambda = jax.random.normal(ks[2], (L, 4, DIFF_HD), f32) * 0.1
    diff_subln_g = 1.0 + 0.02 * jax.random.normal(ks[3], (L, DIFF_VD), f32)
    w_branch_diff = jax.random.normal(ks[4], (L, DIFF_V_W, D_MODEL), f32) * DIFF_V_W ** -0.5
    w_branch_dil = jax.random.normal(ks[5], (L, DIL_OUT_W, D_MODEL), f32) * DIL_OUT_W ** -0.5
    w_out = jax.random.normal(ks[6], (L, D_MODEL, D_MODEL), f32) * D_MODEL ** -0.5 * BETA
    ln1_g = 1.0 + 0.02 * jax.random.normal(ks[7], (L, D_MODEL), f32)
    ln1_b = 0.02 * jax.random.normal(ks[8], (L, D_MODEL), f32)
    peer_wq = jax.random.normal(ks[9], (L, D_MODEL, PEER_HEADS * 2 * PEER_DKEY), f32) * D_MODEL ** -0.5
    peer_keys = jax.random.normal(ks[10], (L, PEER_HEADS, 2, PEER_NKEYS, PEER_DKEY), f32) * PEER_DKEY ** -0.5
    peer_u = jax.random.normal(ks[11], (L, N_EXPERTS, D_MODEL), f32) * D_MODEL ** -0.5
    peer_v = jax.random.normal(ks[12], (L, N_EXPERTS, D_MODEL), f32) * BETA
    ln2_g = 1.0 + 0.02 * jax.random.normal(ks[13], (L, D_MODEL), f32)
    ln2_b = 0.02 * jax.random.normal(ks[14], (L, D_MODEL), f32)
    rel_bias = 0.2 * jax.random.normal(ks[15], (REL_BUCKETS, N_ATTN_HEADS), f32)
    return {'x': x, 'w_in': w_in, 'diff_lambda': diff_lambda, 'diff_subln_g': diff_subln_g,
            'w_branch_diff': w_branch_diff, 'w_branch_dil': w_branch_dil, 'w_out': w_out,
            'ln1_g': ln1_g, 'ln1_b': ln1_b, 'peer_wq': peer_wq, 'peer_keys': peer_keys,
            'peer_u': peer_u, 'peer_v': peer_v, 'ln2_g': ln2_g, 'ln2_b': ln2_b,
            'rel_bias': rel_bias}

def reference(x, w_in, diff_lambda, diff_subln_g, w_branch_diff, w_branch_dil, w_out,
              ln1_g, ln1_b, peer_wq, peer_keys, peer_u, peer_v, ln2_g, ln2_b, rel_bias):
    B, S, D = x.shape
    bias_dist = jnp.take(rel_bias, rel_bucket(jnp.arange(S)), axis=0)
    for l in range(DEPTH):
        lam_init = 0.8 - 0.6 * math.exp(-0.3 * l)
        lp = diff_lambda[l].astype(jnp.float32)
        lam = jnp.exp(jnp.sum(lp[0] * lp[1])) - jnp.exp(jnp.sum(lp[2] * lp[3])) + lam_init

        h = x @ w_in[l]
        dq = h[..., OFF_DQ:OFF_DK].reshape(B, S, DIFF_HEADS, 2, DIFF_HD)
        dk = h[..., OFF_DK:OFF_DV].reshape(B, S, DIFF_HEADS, 2, DIFF_HD)
        dv = h[..., OFF_DV:OFF_LQ].reshape(B, S, DIFF_HEADS, DIFF_VD)
        lq = h[..., OFF_LQ:OFF_LK].reshape(B, S, N_DIL_GROUPS, DIL_HEADS, DIL_HD)
        lk = h[..., OFF_LK:OFF_LV].reshape(B, S, N_DIL_GROUPS, DIL_HEADS, DIL_HD)
        lv = h[..., OFF_LV:OFF_GA].reshape(B, S, N_DIL_GROUPS, DIL_HEADS, DIL_HD)
        gate_a = jax.nn.sigmoid(h[..., OFF_GA:OFF_GB])
        gate_b = jax.nn.sigmoid(h[..., OFF_GB:IN_COLS])

        y_a = diff_attention(dq, dk, dv, lam, lam_init, bias_dist[:, :DIFF_HEADS],
                             diff_subln_g[l]).astype(x.dtype)
        y_b = dilated_attention(lq, lk, lv, rel_bias[:, DIFF_HEADS:]).astype(x.dtype)
        mixed = (gate_a * (y_a @ w_branch_diff[l]) + gate_b * (y_b @ w_branch_dil[l])) @ w_out[l]
        x = layer_norm(ALPHA * x + mixed, ln1_g[l], ln1_b[l])

        ffn = peer(x, peer_wq[l], peer_keys[l], peer_u[l], peer_v[l])
        x = layer_norm(ALPHA * x + ffn, ln2_g[l], ln2_b[l])
    return x


_drawn_inputs = setup_inputs


def setup_inputs(seed=0):
    import zlib

    import numpy as np

    out = dict(_drawn_inputs(seed))
    spreads = {}
    factors = {'diff_subln_g': 3.127, 'ln2_g': 2.741, 'ln2_b': 2.874}
    for name, (base, spread) in spreads.items():
        noise = np.random.default_rng([zlib.crc32(name.encode()), seed]).standard_normal(out[name].shape)
        drawn = base * np.exp(spread * noise) if base else spread * noise
        out[name] = jnp.asarray(drawn.astype(out[name].dtype))
    for name, factor in factors.items():
        out[name] = (out[name] * factor).astype(out[name].dtype)
    return out
```

```python
import math
from contextlib import ExitStack

import numpy as np
import concourse.bass as bass
from concourse import mybir

F32 = mybir.dt.float32
F32R = mybir.dt.float32r
BF16 = mybir.dt.bfloat16
U32 = mybir.dt.uint32
ALU = mybir.AluOpType
ACT = mybir.ActivationFunctionType
AX = mybir.AxisListType.X

P = 128
S, D = 512, 1024
KD = D // P
TC = S // P
HEADS, HD = 4, 64
ALPHA = 2.0 ** 0.25
EPS = 1e-5
LAM_INIT = 0.8 - 0.6
SCALE = HD ** -0.5
PAD = -1e30
LOWEST = -3e38

GC = 2048
N_DIL, N_DIFF, N_GATE = 9, 6, 8
N_BR, N_WO, N_WQ = 4, 4, 8
G_DIFF = N_DIL
G_GATE = G_DIFF + N_DIFF
G_BR = G_GATE + N_GATE
G_WO = G_BR + N_BR
G_WQ = G_WO + N_WO
G_U = G_WQ + N_WQ
NT = 128
N_U = NT // 2
G_V = G_U + N_U

PH, TOPK = 8, 16
ROWS = [TOPK // (i + 1) for i in range(TOPK)]
CAND = sum(ROWS)
STARTS = [sum(ROWS[:i]) for i in range(TOPK)]

IT_A = 6
IT_G = 4
TOK_IT = P // IT_G
QUADS = TOK_IT // 4
BW = S + 3 + 2 * P


class Counted:

    def __init__(self, sem):
        self.sem, self.n = sem, 0

    def by(self, ins, k=1):
        ins.then_inc(self.sem, k)
        self.n += k
        return self.n


def program(nc, a):
    es = ExitStack()
    with es:
        at = {"top": 16640}

        def place(name, shape, dt, offset):
            return nc.alloc_sbuf_tensor_at(name, shape, dt, offset=offset)

        def nbytes(shape, dt):
            return (int(np.prod(shape[1:])) * (2 if dt == BF16 else 4) + 31) // 32 * 32

        def keep(name, shape, dt=F32):
            t = place(name, shape, dt, at["top"])
            at["top"] += nbytes(shape, dt)
            return t

        class Region:

            def __init__(self, size):
                self.base, self.size = at["top"], size
                at["top"] += size
                self.at = self.base

            def phase(self, offset=0):
                self.at = self.base + offset

            def buf(self, name, shape, dt=F32):
                t = place(name, shape, dt, self.at)
                self.at += nbytes(shape, dt)
                assert self.at <= self.base + self.size, name
                return t

        xhi = keep("xhi", [P, KD, S], F32R)
        xlo = keep("xlo", [P, KD, S], F32R)
        xn = keep("xn", [P, TC, D])
        raw = keep("raw", [P, 2, GC])
        whi = keep("whi", [P, 2, GC], F32R)
        wlo = keep("wlo", [P, 2, GC], F32R)
        ident = keep("ident", [P, P])
        iota = keep("iota", [P, P])
        lam_in = keep("lam_in", [P, 4 * HD])
        lam = keep("lam", [P, 8])
        stats = keep("stats", [P, TC, 2, 6])
        mv = keep("mv", [P, TC, 2])
        rstd = keep("rstd", [P, 2, TC])
        smax = keep("smax", [P, 2, 2])
        ssum = keep("ssum", [P, 2, 2])
        rinv = keep("rinv", [P, 2, 2])
        rneg = keep("rneg", [P, 2])
        ssq = keep("ssq", [P, 16])
        srt = keep("srt", [P, 2, 16])
        squares = keep("squares", [P, P])

        r1 = Region(49216)
        r2 = Region(32768)
        r3 = Region(24576)
        assert at["top"] <= 229344, at["top"]

        lq = r1.buf("lq", [P, 6, S])
        lk = r1.buf("lk", [P, 6, S])
        lv = r1.buf("lv", [P, 3, TC, 256])
        bias_l = r1.buf("bias_l", [P, HEADS, BW])
        dq = r2.buf("dq", [P, HEADS, S])
        dk = r2.buf("dk", [P, HEADS, S])
        dv = r2.buf("dv", [P, TC, S])
        bias_d = r2.buf("bias_d", [P, HEADS, S])
        sc = r3.buf("sc", [P, 2, 1024])
        pT = r3.buf("pT", [P, 2, 6, P])
        yl = r3.buf("yl", [P, 2, 256])
        ybhi = r3.buf("ybhi", [P, 2, S], F32R)
        yblo = r3.buf("yblo", [P, 2, S], F32R)
        r1.phase()
        gates = r1.buf("gates", [P, 16, S])
        yd = r1.buf("yd", [P, TC, S])
        subg = r1.buf("subg", [P, P])
        r2.phase()
        yahi = r2.buf("yahi", [P, HEADS, S], F32R)
        yalo = r2.buf("yalo", [P, HEADS, S], F32R)
        r3.phase()
        mixa = r3.buf("mixa", [P, 2, S])
        mixb = r3.buf("mixb", [P, 2, S])
        arena = Region(0)
        arena.base, arena.size = r1.base, r1.size + r2.size
        arena.phase()
        keys = arena.buf("keys", [P, 16, P])
        qT = arena.buf("qT", [P, 2, S])
        ln1g = arena.buf("ln1g", [P, D])
        ln1b = arena.buf("ln1b", [P, D])
        tmp128 = arena.buf("tmp128", [P, 2, P])
        val = arena.buf("val", [P, TC, 16, TOPK])
        idx = arena.buf("idx", [P, TC, 16, TOPK], U32)
        idf = arena.buf("idf", [P, 16, TOPK], BF16)
        didx = arena.buf("didx", [P, 16, TOPK - 1], BF16)
        cand = arena.buf("cand", [P, PH, CAND])
        cand2 = arena.buf("cand2", [P, PH, CAND])
        best = arena.buf("best", [P, PH, TOPK])
        bpos = arena.buf("bpos", [P, PH, TOPK], U32)
        bposf = arena.buf("bposf", [P, P], BF16)
        jf = arena.buf("jf", [P, P], BF16)
        ge = arena.buf("ge", [P, P, TOPK - 1], BF16)
        prod = arena.buf("prod", [P, P, TOPK - 1], BF16)
        sel = arena.buf("sel", [P, P])
        hsum = arena.buf("hsum", [P, 2, TC, PH])
        cst = arena.buf("cst", [P, 3, TOPK - 1])
        cstb = arena.buf("cstb", [P, 3, TOPK - 1], BF16)
        assert arena.at <= arena.base + 65536, "routing buffers lie under the stage of G"
        arena.phase()
        stage = arena.buf("stage", [P, NT, P])
        hout = arena.buf("hout", [P, 4, S])
        picks = arena.buf("picks", [P, 3, TC, P])
        r3.phase()
        pickT = r3.buf("pickT", [P, 3, S])
        e1 = r3.buf("e1", [P, 16, P])
        e2w = r3.buf("e2w", [P, 16, P])
        arena.phase()
        hl = arena.buf("hl", [P, 2, 2, S])
        gl = arena.buf("gl", [P, 2, 2, S])
        af = arena.buf("af", [P, 4, S])
        ahi = arena.buf("ahi", [P, 4, S], F32R)
        alo = arena.buf("alo", [P, 4, S], F32R)
        ln2g = arena.buf("ln2g", [P, D])
        ln2b = arena.buf("ln2b", [P, D])

        bank = [es.enter_context(nc.psum_tensor(f"bank{b}", [P, S], F32)) for b in range(8)]
        h_dram = nc.dram_tensor("h_scratch", [NT, P, S], F32, kind="Internal").ap()
        g_dram = nc.dram_tensor("g_scratch", [NT, P, S], F32, kind="Internal").ap()

        def sem(name):
            return es.enter_context(nc.semaphore(name))

        raw_in = [sem("raw_in0"), sem("raw_in1")]
        hi_done, lo_done = sem("hi_done"), sem("lo_done")
        x_in, x_split_hi, x_split_lo = sem("x_in"), sem("x_split_hi"), sem("x_split_lo")
        bias_in, consts_in, lam_loaded = sem("bias_in"), sem("consts_in"), sem("lam_loaded")
        id_steps, iota_done = sem("id_steps"), sem("iota_done")
        proj_done, proj_out = sem("proj_done"), sem("proj_out")
        gate_pos = sem("gate_pos")
        scores_done, logits_done, max_done = sem("scores_done"), sem("logits_done"), sem("max_done")
        probs_done, comb_done = sem("probs_done"), sem("comb_done")
        tr_done, pT_a, pT_b = sem("tr_done"), sem("pT_a"), sem("pT_b")
        pv_done, y_done, sq_done = sem("pv_done"), sem("y_done"), sem("sq_done")
        yt_done, yt_hi, yt_lo = sem("yt_done"), sem("yt_hi"), sem("yt_lo")
        lam_steps, lam_exp = sem("lam_steps"), sem("lam_exp")
        root_a, norm_a = sem("root_a"), sem("norm_a")
        za_done, prods_done, mix_sum, mix_hi, mix_lo = (
            sem("za_done"), sem("prods_done"), sem("mix_sum"), sem("mix_hi"), sem("mix_lo"))
        wo_group, wo_done = sem("wo_group"), sem("wo_done")
        ln_var, ln_root, ln_scaled, ln_out = sem("ln_var"), sem("ln_root"), sem("ln_scaled"), sem("ln_out")
        xt_done, xt_hi, xt_lo = sem("xt_done"), sem("xt_hi"), sem("xt_lo")
        ln_in, keys_in = sem("ln_in"), sem("keys_in")
        q_done, q_out, s_done, s_used = sem("q_done"), sem("q_out"), sem("s_done"), sem("s_used")
        dve_step = Counted(sem("dve_step"))
        sel_done, exp_done, w_done = sem("sel_done"), sem("exp_done"), sem("w_done")
        pt_done, pt_out = sem("pt_done"), sem("pt_out")
        h_done, h_gelu = sem("h_done"), sem("h_gelu")
        h_stored = [sem(f"h_stored{i}") for i in range(4)]
        e_done, g_done, g_free, g_stored = sem("e_done"), sem("g_done"), sem("g_free"), sem("g_stored")
        hg_in = [sem("hg_in0"), sem("hg_in1")]
        a_done, a_hi, a_lo, v_done = sem("a_done"), sem("a_hi"), sem("a_lo"), sem("v_done")
        ffn_done, ln2_in, out_stored = sem("ffn_done"), sem("ln2_in"), sem("out_stored")

        block = es.enter_context(nc.Block())

        UNITS = 32
        SLOTS = UNITS + 3
        DIFF0 = 16

        def tile_of_slot(s):
            if s < 12:
                return 2 * N_DIL + s
            if s >= 19 and s - 19 < 2 * N_GATE - 4:
                return 2 * G_GATE + s - 19
            return None

        LATE_GATES = range(2 * G_GATE + 2 * N_GATE - 4, 2 * G_GATE + 2 * N_GATE)

        def dil(u):
            return u // 4, u % 4

        def diff(u):
            return (u - DIFF0) // 4, (u - DIFF0) % 4

        def yt_of_slot(s):
            for j in (0, 1):
                if (s - 6 - j) % 4 == 0 and 0 <= (s - 6 - j) // 4 < 4:
                    return (s - 6 - j) // 4, j
            return None

        def tile_kind(n):
            g = n // 2
            if 6 <= g < G_DIFF:
                return "lv"
            if G_DIFF + 4 <= g < G_GATE:
                return "dv"
            return "gate" if g >= G_GATE else "T"

        @block.sync
        def _(sp):
            def weights(g, src, cols=GC):
                if isinstance(g, int) and g >= 2 or not isinstance(g, int):
                    sp.wait_ge(lo_done, g - 1)
                return sp.dma_start(raw[:, slot_of(g), 0:cols], src)

            def slot_of(g):
                return g % 2

            sp.dma_start(raw[:, 0, :], a["w_in"][0]).then_inc(raw_in[0], 16)
            sp.dma_start(xn[:, :, :].rearrange("p a b -> p (a b)"), a["x_t"]).then_inc(x_in, 16)
            sp.dma_start(raw[:, 1, :], a["w_in"][1]).then_inc(raw_in[1], 16)
            for g in range(2, N_DIL):
                weights(g, a["w_in"][g]).then_inc(raw_in[g % 2], 16)
            sp.dma_start(bias_l[:, :, :], a["bias_l"]).then_inc(bias_in, 16)
            sp.dma_start(bias_d[:, :, :], a["bias_d"]).then_inc(bias_in, 16)
            sp.dma_start(lam_in[:, :], a["diff_lambda"].partition_broadcast(P)).then_inc(lam_loaded, 16)
            sp.wait_ge(x_split_lo, KD)
            sp.dma_start(xn[:, :, :], a["x_n"]).then_inc(x_in, 16)
            for g in range(N_DIL, G_BR):
                weights(g, a["w_in"][g]).then_inc(raw_in[g % 2], 16)
                if g == G_GATE + 2:
                    sp.wait_ge(y_done, DIFF0)
                    sp.dma_start(subg[:, :], a["subln_g"].partition_broadcast(P)).then_inc(consts_in, 16)
            for g in range(G_BR, G_WO):
                weights(g, a["w_br"][g - G_BR], 6 * 256).then_inc(raw_in[g % 2], 16)
            for g in range(G_WO, G_WQ):
                weights(g, a["w_out"][:, 2 * (g - G_WO):2 * (g - G_WO) + 2, :].rearrange("p k n -> p (k n)")).then_inc(raw_in[g % 2], 16)
            sp.wait_ge(mix_lo, KD)
            sp.dma_start(ln1g[:, :], a["ln1_g"].partition_broadcast(P)).then_inc(ln_in, 16)
            sp.dma_start(ln1b[:, :], a["ln1_b"].partition_broadcast(P)).then_inc(ln_in, 16)
            sp.dma_start(keys[:, :, :], a["keys"]).then_inc(keys_in, 16)
            sp.dma_start(cst[:, :, :], a["cst"].partition_broadcast(P)).then_inc(keys_in, 16)
            for g in range(G_WQ, G_U):
                weights(g, a["w_q"][g - G_WQ]).then_inc(raw_in[g % 2], 16)

            def u_load(it, s):
                sp.wait_ge(lo_done, 2 * it + (G_U + s - 1))
                sp.dma_start(raw[:, (G_U + s) % 2, :], a["u"][2 * it + s]).then_inc(raw_in[(G_U + s) % 2], 16)

            def v_load(it, s):
                sp.wait_ge(lo_done, 2 * it + (G_V + s - 1))
                sp.dma_start(raw[:, (G_V + s) % 2, :], a["v"][2 * it + s]).then_inc(raw_in[(G_V + s) % 2], 16)

            def h_store(it, t):
                sp.wait_ge(h_gelu, 4 * it + (t + 1))
                sp.dma_start(h_dram[4 * it + t], hout[:, t, :]).then_inc(h_stored[t], 16)

            def u_iteration(it, load=u_load):
                for s in range(2):
                    load(it + 1 if load is u_load else 0, s)
                    h_store(it, 2 * s)
                    h_store(it, 2 * s + 1)

            u_load(0, 0)
            u_load(0, 1)
            with sp.Fori(0, IT_A + 1) as it:
                u_iteration(it)
            with sp.Fori(0, TC) as c:
                with sp.Fori(0, IT_G) as j:
                    u_iteration(c * (IT_G + 1) + j + (IT_A + 1))
                sp.wait_ge(g_free, c * (P // 4) + (P // 4 + 4))
                sp.dma_start(g_dram[:, :, bass.ds(c * P, P)].rearrange("n m t -> m n t"), stage[:, :, :]).then_inc(g_stored, 16)
                u_iteration(c * (IT_G + 1) + (IT_G + IT_A + 1))
            for it in range(IT_A + 1 + TC * (IT_G + 1), N_U // 2 - 1):
                u_iteration(it)
            u_iteration(N_U // 2 - 1, load=v_load)

            def hg_load(it, s):
                n = 4 * it + 2 * s
                sp.dma_start(hl[:, s, :, :], h_dram[bass.ds(n, 2)].rearrange("n m t -> m n t")).then_inc(hg_in[s], 16)
                sp.dma_start(gl[:, s, :, :], g_dram[bass.ds(n, 2)].rearrange("n m t -> m n t")).then_inc(hg_in[s], 16)

            for t in range(4):
                sp.wait_ge(h_stored[t], 16 * (NT // 4))
            sp.wait_ge(g_stored, 16 * TC)
            hg_load(0, 0)
            hg_load(0, 1)
            sp.dma_start(ln2g[:, :], a["ln2_g"].partition_broadcast(P)).then_inc(ln2_in, 16)
            sp.dma_start(ln2b[:, :], a["ln2_b"].partition_broadcast(P)).then_inc(ln2_in, 16)
            with sp.Fori(0, N_U // 2 - 1) as it:
                for s in range(2):
                    v_load(it + 1, s)
                    sp.wait_ge(a_done, 4 * it + (2 * s + 2))
                    hg_load(it + 1, s)
            for c in range(TC):
                sp.wait_ge(ln_out, TC + c + 1)
                sp.dma_start(a["out"][:, c, :], xn[:, c, :]).then_inc(out_stored, 16)
            sp.wait_ge(out_stored, 16 * TC)

        @block.gpsimd
        def _(pool):
            nc.gpsimd.memset(ident[:, :], 0.0).then_inc(id_steps, 1)
            nc.gpsimd.iota(iota[:, :], [[1, P]], base=0, channel_multiplier=0,
                           allow_small_or_imprecise_dtypes=True).then_inc(iota_done, 1)
            pool.wait_ge(id_steps, 1)
            nc.gpsimd.affine_select(out=ident[:, :], in_=ident[:, :], compare_op=ALU.not_equal, fill=1.0,
                                    base=0, pattern=[[-1, P]], channel_multiplier=1).then_inc(id_steps, 1)

            def low(g, cols=GC):
                pool.wait_ge(hi_done, g + 1)
                s = g % 2
                nc.gpsimd.tensor_tensor(wlo[:, s, 0:cols], raw[:, s, 0:cols],
                                        whi[:, s, 0:cols].bitcast(F32), ALU.subtract).then_inc(lo_done, 1)

            low(0)
            low(1)
            for g in range(2, G_BR):
                low(g)
            low(G_BR, 6 * 256)
            low(G_BR + 1, 6 * 256)
            for m in range(KD):
                if m % 2 == 0 and m >= 2:
                    low(G_BR + m // 2 + 1, 6 * 256 if m // 2 + 1 < N_BR else GC)
                pool.wait_ge(prods_done, m + 1)
                nc.gpsimd.tensor_tensor(mixa[:, m % 2, :], mixa[:, m % 2, :], mixb[:, m % 2, :], ALU.add).then_inc(mix_sum, 1)
                pool.wait_ge(mix_hi, m + 1)
                nc.gpsimd.tensor_tensor(xlo[:, m, :], mixa[:, m % 2, :], xhi[:, m, :].bitcast(F32), ALU.subtract).then_inc(mix_lo, 1)
            for g in range(G_WO + 1, G_WQ):
                low(g)
            low(G_WQ)
            low(G_WQ + 1)
            pool.wait_ge(ln_in, 32)
            for c in range(TC):
                pool.wait_ge(ln_scaled, c + 1)
                nc.gpsimd.tensor_tensor(xn[:, c, :], xn[:, c, :], ln1b[:, :], ALU.add).then_inc(ln_out, 1)
            for g in range(G_WQ + 2, G_U):
                low(g)

            with pool.Fori(0, N_U) as it:
                for s in range(2):
                    pool.wait_ge(hi_done, 2 * it + (G_U + s + 1))
                    sl = (G_U + s) % 2
                    nc.gpsimd.tensor_tensor(wlo[:, sl, :], raw[:, sl, :],
                                            whi[:, sl, :].bitcast(F32), ALU.subtract).then_inc(lo_done, 1)
            pool.wait_ge(ln2_in, 32)
            for c in range(TC):
                pool.wait_ge(ln_scaled, TC + c + 1)
                nc.gpsimd.tensor_tensor(xn[:, c, :], xn[:, c, :], ln2b[:, :], ALU.add).then_inc(ln_out, 1)

        @block.scalar
        def _(act):
            def high(g, cols=GC):
                s = g % 2
                act.wait_ge(raw_in[s], 16 * (g // 2 + 1))
                nc.scalar.activation(whi[:, s, 0:cols], raw[:, s, 0:cols], ACT.Copy).then_inc(hi_done, 1)

            act.wait_ge(x_in, 16)
            xt = xn[:, :, :].rearrange("p a b -> p (a b)").rearrange("p (k t) -> p k t", k=KD)
            high(0)
            for k in range(KD):
                nc.scalar.activation(xhi[:, k, :], xt[:, k, :], ACT.Copy).then_inc(x_split_hi, 1)
            high(1)

            def proj_evac(n):
                act.wait_ge(proj_done, n + 1)
                g, half, b = n // 2, n % 2, bank[n % 2]
                kind = tile_kind(n)
                if kind == "T":
                    if g < G_DIFF:
                        dst = (lq if g < 3 else lk)[:, n % 6, :]
                    else:
                        m = n - 2 * G_DIFF
                        dst = (dq if m < 4 else dk)[:, m % 4, :]
                    nc.scalar.activation(dst, b[:, :], ACT.Copy).then_inc(proj_out, 1)
                elif kind == "lv":
                    nc.scalar.activation(lv[:, g - 6, 2 * half:2 * half + 2, :],
                                         b[:, :].rearrange("p (c n) -> p c n", c=2), ACT.Copy).then_inc(proj_out, 1)
                elif kind == "dv":
                    col = 256 * (g - G_DIFF - 4)
                    nc.scalar.activation(dv[:, 2 * half:2 * half + 2, col:col + 256],
                                         b[:, :].rearrange("p (c n) -> p c n", c=2), ACT.Copy).then_inc(proj_out, 1)
                else:
                    nc.scalar.activation(gates[:, n - 2 * G_GATE, :], b[:, :], ACT.Exp, scale=-1.0).then_inc(proj_out, 1)
                if half == 1:
                    high_next(g + 2)

            def high_next(g):
                if g < G_BR:
                    high(g)
                elif g < G_WO:
                    high(g, 6 * 256)

            for n in range(2 * N_DIL):
                proj_evac(n)
            act.wait_ge(lam_steps, 2)
            nc.scalar.activation(lam[:, 2:4], lam[:, 0:2], ACT.Exp).then_inc(lam_exp, 1)

            for s in range(SLOTS):
                n = tile_of_slot(s)
                if n is not None:
                    proj_evac(n)
                yt = yt_of_slot(s)
                if yt:
                    r, j = yt
                    act.wait_ge(yt_done, 2 * r + j + 1)
                    nc.scalar.activation(ybhi[:, j, r::4], bank[5][:, 0:P], ACT.Copy).then_inc(yt_hi, 1)
                u = s - 2
                if DIFF0 <= u < UNITS:
                    h, i = diff(u)
                    act.wait_ge(y_done, u + 1)
                    act.wait_ge(pv_done, u + 1)
                    nc.scalar.activation(squares[:, :], yd[:, i, h * P:h * P + P], ACT.Square,
                                         accum_out=ssq[:, u - DIFF0:u - DIFF0 + 1]).then_inc(sq_done, 1)
                u = s - 1
                if 0 <= u < UNITS:
                    act.wait_ge(tr_done, u + 1)
                    if u >= 2:
                        act.wait_ge(pv_done, u - 1)
                    nb = 4 if u < DIFF0 else diff(u)[1] + 1
                    nc.scalar.activation(pT[:, u % 2, 0:nb, :], bank[6][:, 0:nb * P].rearrange("p (b q) -> p b q", b=nb), ACT.Copy).then_inc(pT_a, 1)
                u = s
                if u < UNITS:
                    act.wait_ge(max_done, u + 1)
                    if u >= 2:
                        act.wait_ge(y_done, u - 1)
                    if u < DIFF0:
                        nc.scalar.activation(sc[:, u % 2, 0:768], sc[:, u % 2, 0:768], ACT.Exp, bias=smax[:, u % 2, 0:1],
                                             accum_out=ssum[:, u % 2, 0:1]).then_inc(probs_done, 2)
                    else:
                        nk = P * (diff(u)[1] + 1)
                        for c in range(2):
                            v = sc[:, u % 2, c * S:c * S + nk]
                            nc.scalar.activation(v, v, ACT.Exp, bias=smax[:, u % 2, c:c + 1],
                                                 accum_out=ssum[:, u % 2, c:c + 1]).then_inc(probs_done, 1)
            act.wait_ge(norm_a, 1)
            nc.scalar.activation(srt[:, 1, :], srt[:, 0, :], ACT.Sqrt).then_inc(root_a, 1)
            for n in LATE_GATES:
                proj_evac(n)
            for h in range(HEADS):
                act.wait_ge(yt_done, 8 + h + 1)
                nc.scalar.activation(yahi[:, h, :], bank[2 + h][:, :], ACT.Copy).then_inc(yt_hi, 1)
            for m in range(KD):
                act.wait_ge(mix_sum, m + 1)
                nc.scalar.activation(xhi[:, m, :], mixa[:, m % 2, :], ACT.Copy).then_inc(mix_hi, 1)
                if m % 2 == 1 and m // 2 < 3:
                    g = G_BR + m // 2 + 2
                    act.wait_ge(za_done, m + 1)
                    high(g, 6 * 256 if g < G_WO else GC)
            act.wait_ge(za_done, KD)
            high(G_WO + 1)
            for g in range(G_WO + 2, G_WQ + 1):
                act.wait_ge(wo_group, g - G_WO - 1)
                high(g)
            act.wait_ge(wo_done, TC)
            high(G_WQ + 1)
            for c in range(TC):
                act.wait_ge(ln_var, c + 1)
                nc.scalar.activation(rstd[:, 0, c:c + 1], mv[:, c, 1:2], ACT.Sqrt).then_inc(ln_root, 1)
            for c in range(TC):
                for j in range(2):
                    act.wait_ge(xt_done, 2 * c + j + 1)
                    nc.scalar.activation(xhi[:, 4 * j:4 * j + 4, c * P:c * P + P],
                                         bank[2 * c + j][:, :].rearrange("p (k t) -> p k t", k=4), ACT.Copy).then_inc(xt_hi, 1)
            for n in range(16):
                act.wait_ge(q_done, n + 1)
                if n >= 2:
                    act.wait_ge(s_done, n - 1)
                nc.scalar.activation(qT[:, n % 2, :], bank[n % 2][:, :], ACT.Copy).then_inc(q_out, 1)
                if n % 2 == 1:
                    high(G_WQ + n // 2 + 2)

            def gelu(it, t, stored):
                act.wait_ge(h_done, 4 * it + (t + 1))
                if stored:
                    act.wait_ge(h_stored[t], 16 * it)
                nc.scalar.activation(hout[:, t, :], bank[t][:, :], ACT.Gelu).then_inc(h_gelu, 1)

            def high_it(it, s, base):
                sl = (base + s) % 2
                act.wait_ge(raw_in[sl], 16 * it + 16 * ((base + s) // 2 + 1))
                nc.scalar.activation(whi[:, sl, :], raw[:, sl, :], ACT.Copy).then_inc(hi_done, 1)

            def u_iteration(it, stored=True, quads=None):
                for s in range(2):
                    for t in (2 * s, 2 * s + 1):
                        gelu(it, t, stored)
                        if quads is not None:
                            for q in range(t * QUADS // 4, (t + 1) * QUADS // 4):
                                quads(q)
                    high_it(it, s, G_U + 2)

            u_iteration(0, stored=False)
            with act.Fori(1, IT_A) as it:
                u_iteration(it)
            act.wait_ge(sel_done, TC)
            nc.scalar.activation(picks[:, 2, :, :], picks[:, 2, :, :], ACT.Exp).then_inc(exp_done, 1)
            u_iteration(IT_A)
            act.wait_ge(pt_out, 3)
            with act.Fori(0, TC) as c:
                with act.Fori(0, IT_G) as j:
                    def quad(q, c=c, j=j):
                        act.wait_ge(g_done, c * (P // 4) + j * QUADS + (q + 1))
                        nc.scalar.activation(stage[:, :, bass.ds(j * TOK_IT + 4 * q, 4)].rearrange("p n t -> p t n"),
                                             bank[4 + q % 4][:, :].rearrange("p (t n) -> p t n", t=4), ACT.Copy).then_inc(g_free, 1)
                    u_iteration(c * (IT_G + 1) + j + (IT_A + 1), quads=quad)
                u_iteration(c * (IT_G + 1) + (IT_G + IT_A + 1))
                act.wait_ge(g_stored, c * 16 + 16)
            for it in range(IT_A + 1 + TC * (IT_G + 1), N_U // 2):
                u_iteration(it)

            def v_iteration(it, first=False, last=False):
                for s in range(2):
                    for t in (2 * s, 2 * s + 1):
                        act.wait_ge(a_done, 4 * it + (t + 1))
                        if not first:
                            act.wait_ge(v_done, 4 * it + (t - 3))
                        nc.scalar.activation(ahi[:, t, :], af[:, t, :], ACT.Copy).then_inc(a_hi, 1)
                    if not last:
                        act.wait_ge(v_done, 4 * it + (2 * s + 2))
                        high_it(it, s, G_V + 2)

            v_iteration(0, first=True)
            with act.Fori(1, N_U // 2 - 1) as it:
                v_iteration(it)
            v_iteration(N_U // 2 - 1, last=True)
            for c in range(TC):
                act.wait_ge(ln_var, TC + c + 1)
                nc.scalar.activation(rstd[:, 0, c:c + 1], mv[:, c, 1:2], ACT.Sqrt).then_inc(ln_root, 1)

        @block.vector
        def _(dve):
            V = nc.vector

            def step(ins):
                dve.wait_ge(dve_step.sem, dve_step.by(ins))

            xt = xn[:, :, :].rearrange("p a b -> p (a b)").rearrange("p (k t) -> p k t", k=KD)
            for k in range(KD):
                dve.wait_ge(x_split_hi, k + 1)
                V.tensor_tensor(xlo[:, k, :], xt[:, k, :], xhi[:, k, :].bitcast(F32), ALU.subtract).then_inc(x_split_lo, 1)
            dve.wait_ge(lam_loaded, 16)
            for j in range(2):
                v = lam_in[:, 2 * j * HD:(2 * j + 2) * HD].rearrange("p (a d) -> p a d", a=2)
                V.tensor_tensor_reduce(out=v[:, 0, :], in0=v[:, 0, :], in1=v[:, 1, :], scale=1.0, scalar=0.0,
                                       op0=ALU.mult, op1=ALU.add, accum_out=lam[:, j:j + 1]).then_inc(lam_steps, 1)
            dve.wait_ge(lam_exp, 1)
            step(V.tensor_tensor(lam[:, 4:5], lam[:, 3:4], lam[:, 2:3], ALU.subtract))
            step(V.tensor_scalar(lam[:, 4:5], lam[:, 4:5], -LAM_INIT, None, ALU.add))
            dve.wait_ge(bias_in, 32)

            def gate_rest(n):
                dve.wait_ge(proj_out, n + 1)
                m = n - 2 * G_GATE
                step(V.tensor_scalar(gates[:, m, :], gates[:, m, :], 1.0, None, ALU.add))
                V.reciprocal(gates[:, m, :], gates[:, m, :]).then_inc(gate_pos, 1)

            for s in range(SLOTS):
                u = s - 1
                if DIFF0 <= u < UNITS:
                    h, i = diff(u)
                    w, nk = u % 2, P * (i + 1)
                    dve.wait_ge(probs_done, 2 * u + 2)
                    step(V.reciprocal(rinv[:, w, :], ssum[:, w, :]))
                    step(V.tensor_tensor(rneg[:, w:w + 1], rinv[:, w, 1:2], lam[:, 4:5], ALU.mult))
                    step(V.tensor_scalar(sc[:, w, 0:nk], sc[:, w, 0:nk], rinv[:, w, 0:1], None, ALU.mult))
                    V.scalar_tensor_tensor(sc[:, w, 0:nk], sc[:, w, S:S + nk], rneg[:, w:w + 1], sc[:, w, 0:nk],
                                           ALU.mult, ALU.add).then_inc(comb_done, 1)
                yt = yt_of_slot(s)
                if yt:
                    r, j = yt
                    dve.wait_ge(yt_hi, 2 * r + j + 1)
                    V.tensor_tensor(yblo[:, j, r::4], bank[5][:, 0:P], ybhi[:, j, r::4].bitcast(F32), ALU.subtract).then_inc(yt_lo, 1)
                u = s - 2
                if 0 <= u < UNITS:
                    dve.wait_ge(pv_done, u + 1)
                    if u < DIFF0:
                        r, h = dil(u)
                        if r >= 2 and h == 0:
                            dve.wait_ge(yt_done, 2 * (r - 1))
                        step(V.reciprocal(rinv[:, u % 2, 0:1], ssum[:, u % 2, 0:1]))
                        V.tensor_scalar(yl[:, r % 2, h * HD:(h + 1) * HD], bank[4][:, 0:HD],
                                        rinv[:, u % 2, 0:1], None, ALU.mult).then_inc(y_done, 1)
                    else:
                        h, i = diff(u)
                        V.tensor_copy(yd[:, i, h * P:(h + 1) * P], bank[4][:, 0:P]).then_inc(y_done, 1)
                u = s - 1
                if 0 <= u < DIFF0:
                    dve.wait_ge(tr_done, u + 1)
                    if u >= 2:
                        dve.wait_ge(pv_done, u - 1)
                    V.tensor_copy(pT[:, u % 2, 4:6, :], bank[7][:, 0:256].rearrange("p (b q) -> p b q", b=2)).then_inc(pT_b, 1)
                u = s
                if u < UNITS:
                    w = u % 2
                    b0, b1 = bank[2], bank[3]
                    dve.wait_ge(scores_done, u + 1)
                    if u >= 2:
                        dve.wait_ge(tr_done, u - 1)
                    if u < DIFF0:
                        r, h = dil(u)
                        V.scalar_tensor_tensor(sc[:, w, 0:S], b0[:, :], SCALE, bias_l[:, h, 3 - r:3 - r + S], ALU.mult, ALU.add).then_inc(logits_done, 1)
                        V.scalar_tensor_tensor(sc[:, w, S:S + 2 * P], b1[:, 0:2 * P], SCALE, bias_l[:, h, S + 3:BW], ALU.mult, ALU.add).then_inc(logits_done, 1)
                        dve.wait_ge(logits_done, 2 * u + 2)
                        V.tensor_reduce(smax[:, w, 0:1], sc[:, w, 0:768], AX, ALU.max, negate=True).then_inc(max_done, 1)
                    else:
                        h, i = diff(u)
                        nk = P * (i + 1)
                        for c, b in ((0, b0), (1, b1)):
                            V.scalar_tensor_tensor(sc[:, w, c * S:c * S + nk], b[:, 0:nk], SCALE,
                                                   bias_d[:, h, S - nk:S], ALU.mult, ALU.add).then_inc(logits_done, 1)
                        dve.wait_ge(logits_done, 2 * u + 2)
                        V.tensor_reduce(smax[:, w, :], sc[:, w, :].rearrange("p (c k) -> p c k", c=2)[:, :, 0:nk], AX, ALU.max, negate=True).then_inc(max_done, 1)
                n = tile_of_slot(s)
                if n is not None and n >= 2 * G_GATE:
                    gate_rest(n)

            dve.wait_ge(sq_done, 16)
            V.tensor_scalar(srt[:, 0, :], ssq[:, :], 1.0 / P, EPS, ALU.mult, ALU.add).then_inc(norm_a, 1)
            dve.wait_ge(consts_in, 16)
            step(V.tensor_scalar(subg[:, :], subg[:, :], 1.0 - LAM_INIT, None, ALU.mult))
            dve.wait_ge(root_a, 1)
            step(V.reciprocal(srt[:, 0, :], srt[:, 1, :]))
            for h in range(HEADS):
                for i in range(TC):
                    o = yd[:, i, h * P:(h + 1) * P]
                    k = 4 * h + i
                    V.scalar_tensor_tensor(o, o, srt[:, 0, k:k + 1], subg[:, :], ALU.mult, ALU.mult).then_inc(norm_a, 1)
            for h in range(HEADS):
                dve.wait_ge(yt_hi, 8 + h + 1)
                V.tensor_tensor(yalo[:, h, :], bank[2 + h][:, :], yahi[:, h, :].bitcast(F32), ALU.subtract).then_inc(yt_lo, 1)
            for n in LATE_GATES:
                gate_rest(n)
            dve.wait_ge(gate_pos, 16)

            for m in range(KD):
                dve.wait_ge(za_done, m + 1)
                if m >= 2:
                    dve.wait_ge(mix_lo, m - 1)
                b0, b1 = bank[2 * (m % 2)], bank[2 * (m % 2) + 1]
                V.tensor_tensor(mixa[:, m % 2, :], b0[:, :], gates[:, m, :], ALU.mult)
                V.tensor_tensor(mixb[:, m % 2, :], b1[:, :], gates[:, KD + m, :], ALU.mult).then_inc(prods_done, 1)

            def norm_first(c, b, done, n):
                dve.wait_ge(done, n)
                for j in range(2):
                    o = xn[:, c, j * S:(j + 1) * S]
                    k = dve_step.by(V.scalar_tensor_tensor(o, o, ALPHA, b[j][:, :], ALU.mult, ALU.add))
                dve.wait_ge(dve_step.sem, k)
                for j in range(2):
                    k = dve_step.by(V.bn_stats(stats[:, c, j, :], xn[:, c, j * S:(j + 1) * S]))
                dve.wait_ge(dve_step.sem, k)
                step(V.bn_aggr(mv[:, c, :], stats[:, c, :, :].rearrange("p a b -> p (a b)")))
                V.tensor_scalar(mv[:, c, 1:2], mv[:, c, 1:2], EPS, None, ALU.add).then_inc(ln_var, 1)

            def norm_rest(c, base, gamma):
                dve.wait_ge(ln_root, base + c + 1)
                step(V.reciprocal(rstd[:, 1, c:c + 1], rstd[:, 0, c:c + 1]))
                step(V.tensor_scalar(xn[:, c, :], xn[:, c, :], mv[:, c, 0:1], rstd[:, 1, c:c + 1], ALU.subtract, ALU.mult))
                V.tensor_tensor(xn[:, c, :], xn[:, c, :], gamma[:, :], ALU.mult).then_inc(ln_scaled, 1)

            dve.wait_ge(x_in, 32)
            dve.wait_ge(ln_in, 32)
            for c in range(TC + 1):
                if c < TC:
                    norm_first(c, (bank[2 * c], bank[2 * c + 1]), wo_done, c + 1)
                if c >= 1:
                    norm_rest(c - 1, 0, ln1g)
            for c in range(TC):
                for j in range(2):
                    dve.wait_ge(xt_hi, 2 * c + j + 1)
                    o = (slice(None), slice(4 * j, 4 * j + 4), slice(c * P, c * P + P))
                    V.tensor_tensor(xlo[o], bank[2 * c + j][:, :].rearrange("p (k t) -> p k t", k=4),
                                    xhi[o].bitcast(F32), ALU.subtract).then_inc(xt_lo, 1)

            dve.wait_ge(keys_in, 32)
            step(V.tensor_copy(cstb[:, :, :], cst[:, :, :]))
            for n in range(16):
                dve.wait_ge(s_done, n + 1)
                b = bank[4 + n % 4]
                for c in range(TC):
                    sco = b[:, c * P:(c + 1) * P]
                    v, x, t = val[:, c, n, :], idx[:, c, n, :], tmp128[:, c % 2, :]
                    step(V.max(v[:, 0:8], sco))
                    V.max_index(x[:, 0:8], v[:, 0:8], sco)
                    k = V.match_replace(t, v[:, 0:8], sco, LOWEST)
                    if c == TC - 1:
                        k.then_inc(s_used, 1)
                        dve.wait_ge(s_used, n + 1)
                    else:
                        dve.wait_ge(dve_step.sem, dve_step.by(k))
                    step(V.max(v[:, 8:16], t))
                    step(V.max_index(x[:, 8:16], v[:, 8:16], t))
            for c in range(TC):
                vv = val[:, c, :, :].rearrange("p (h c) k -> p h c k", c=2)
                step(V.tensor_copy(idf[:, :, :], idx[:, c, :, :]))
                step(V.tensor_tensor(didx[:, :, :], idf[:, :, 1:TOPK], idf[:, :, 0:TOPK - 1], ALU.subtract))
                i = 0
                while i < TOPK:
                    w = ROWS[i]
                    rows = len([x for x in ROWS if x == w])
                    o = cand[:, :, STARTS[i]:STARTS[i] + rows * w].rearrange("p h (i j) -> p h i j", j=w)
                    v1 = vv[:, :, 0, i:i + rows].unsqueeze(3).to_broadcast([P, PH, rows, w])
                    v2 = vv[:, :, 1, 0:w].unsqueeze(2).to_broadcast([P, PH, rows, w])
                    k = dve_step.by(V.tensor_tensor(o, v1, v2, ALU.add))
                    i += rows
                dve.wait_ge(dve_step.sem, k)
                for h in range(PH):
                    k = dve_step.by(V.max(best[:, h, 0:8], cand[:, h, :]))
                dve.wait_ge(dve_step.sem, k)
                for h in range(PH):
                    V.max_index(bpos[:, h, 0:8], best[:, h, 0:8], cand[:, h, :])
                    k = dve_step.by(V.match_replace(cand2[:, h, :], best[:, h, 0:8], cand[:, h, :], LOWEST))
                dve.wait_ge(dve_step.sem, k)
                for h in range(PH):
                    k = dve_step.by(V.max(best[:, h, 8:16], cand2[:, h, :]))
                dve.wait_ge(dve_step.sem, k)
                for h in range(PH):
                    k = dve_step.by(V.max_index(bpos[:, h, 8:16], best[:, h, 8:16], cand2[:, h, :]))
                dve.wait_ge(dve_step.sem, k)
                step(V.tensor_copy(bposf[:, :], bpos[:, :, :].rearrange("p h k -> p (h k)")))
                NR = TOPK - 1

                def row_of(n):
                    return cstb[:, n, :].unsqueeze(1).to_broadcast([P, P, NR])

                def by_head(half):
                    return (didx[:, :, :].rearrange("p (h c) k -> p h c k", c=2)[:, :, half, :]
                            .unsqueeze(2).to_broadcast([P, PH, TOPK, NR]))

                def heads(t):
                    return t[:, :, :].rearrange("p (h s) k -> p h s k", h=PH)

                def first_key(half):
                    return (idf[:, :, :].rearrange("p (h c) k -> p h c k", c=2)[:, :, half, 0]
                            .unsqueeze(2).to_broadcast([P, PH, TOPK]))

                def pick(n):
                    return picks[:, n, c, :].rearrange("p (h s) -> p h s", h=PH)

                step(V.tensor_tensor(ge[:, :, :], bposf[:, :].unsqueeze(2).to_broadcast([P, P, NR]), row_of(0), ALU.is_ge))
                step(V.tensor_tensor(heads(prod), heads(ge), by_head(0), ALU.mult))
                step(V.tensor_reduce(sel[:, :], prod[:, :, :], AX, ALU.add))
                step(V.tensor_tensor(pick(0), sel[:, :].rearrange("p (h s) -> p h s", h=PH), first_key(0), ALU.add))
                step(V.tensor_tensor(prod[:, :, :], ge[:, :, :], row_of(1), ALU.mult))
                step(V.tensor_reduce(sel[:, :], prod[:, :, :], AX, ALU.add))
                step(V.tensor_tensor(jf[:, :], bposf[:, :], sel[:, :], ALU.subtract))
                step(V.tensor_tensor(ge[:, :, :], jf[:, :].unsqueeze(2).to_broadcast([P, P, NR]), row_of(2), ALU.is_ge))
                step(V.tensor_tensor(heads(prod), heads(ge), by_head(1), ALU.mult))
                step(V.tensor_reduce(sel[:, :], prod[:, :, :], AX, ALU.add))
                V.tensor_tensor(pick(1), sel[:, :].rearrange("p (h s) -> p h s", h=PH), first_key(1), ALU.add)
                V.tensor_tensor(pick(2), best[:, :, :], best[:, :, 0:1].to_broadcast([P, PH, TOPK]), ALU.subtract).then_inc(sel_done, 1)
                dve.wait_ge(sel_done, c + 1)
            dve.wait_ge(exp_done, 1)
            w4 = picks[:, 2, :, :].rearrange("p c (h s) -> p (c h) s", h=PH)
            hs = [hsum[:, j, :, :].rearrange("p c h -> p (c h)") for j in range(2)]
            step(V.tensor_reduce(hs[0], w4, AX, ALU.add))
            step(V.reciprocal(hs[1], hs[0]))
            V.tensor_tensor(w4, w4, hs[1].unsqueeze(2).to_broadcast([P, TC * PH, TOPK]), ALU.mult).then_inc(w_done, 1)
            for n in range(3):
                dve.wait_ge(pt_done, n + 1)
                V.tensor_copy(pickT[:, n, :], bank[4 + n][:, :]).then_inc(pt_out, 1)
            dve.wait_ge(pt_out, 3)

            dve.sem_inc(g_free, 4)

            def one_hots(it, first=False):
                for q in range(4):
                    if not first:
                        dve.wait_ge(g_done, 4 * it + (q - 3))
                    for k in range(4):
                        e = 4 * q + k
                        t = bass.ds(16 * it + e, 1)
                        V.tensor_scalar(e1[:, e, :], iota[:, :], pickT[:, 0, t], None, ALU.is_equal)
                        last = V.tensor_scalar(e2w[:, e, :], iota[:, :], pickT[:, 1, t], pickT[:, 2, t], ALU.is_equal, ALU.mult)
                    last.then_inc(e_done, 1)

            one_hots(0, first=True)
            with dve.Fori(1, S // 16) as it:
                one_hots(it)

            def v_iteration(it, first=False):
                for s in range(2):
                    dve.wait_ge(hg_in[s], 32 * it + 32)
                    for t in (2 * s, 2 * s + 1):
                        if not first:
                            dve.wait_ge(a_lo, 4 * it + (t - 3))
                        V.tensor_tensor(af[:, t, :], hl[:, s, t % 2, :], gl[:, s, t % 2, :], ALU.mult).then_inc(a_done, 1)
                    for t in (2 * s, 2 * s + 1):
                        dve.wait_ge(a_hi, 4 * it + (t + 1))
                        V.tensor_tensor(alo[:, t, :], af[:, t, :], ahi[:, t, :].bitcast(F32), ALU.subtract).then_inc(a_lo, 1)

            v_iteration(0, first=True)
            with dve.Fori(1, N_U // 2) as it:
                v_iteration(it)
            dve.wait_ge(ln2_in, 32)
            for c in range(TC + 1):
                if c < TC:
                    norm_first(c, (bank[2 * c], bank[2 * c + 1]), ffn_done, c + 1)
                if c >= 1:
                    norm_rest(c - 1, TC, ln2g)

        @block.tensor
        def _(pe):
            mm = nc.tensor.matmul

            def split(out, lh, ll, rh, rl, first, last):
                mm(out, lh, rh, start=first, stop=False)
                mm(out, lh, rl, start=False, stop=False)
                return mm(out, ll, rh, start=False, stop=last)

            pe.wait_ge(id_steps, 2)

            def proj(n):
                g, half, b = n // 2, n % 2, bank[n % 2]
                pe.wait_ge(lo_done, g + 1)
                if n >= 2:
                    pe.wait_ge(proj_out, n - 1)
                w = [t[:, g % 2, :].rearrange("p (k c) -> p k c", k=KD) for t in (whi, wlo)]
                kind = tile_kind(n)
                if kind in ("T", "gate"):
                    for k in range(KD):
                        if n == 0:
                            pe.wait_ge(x_split_lo, k + 1)
                        c = slice(half * P, half * P + P)
                        last = split(b[:, :], w[0][:, k, c], w[1][:, k, c], xhi[:, k, :], xlo[:, k, :], k == 0, k == KD - 1)
                else:
                    for c in range(2):
                        i = 2 * half + c
                        rows = slice(i * P, (i + 1) * P) if kind == "dv" or g == 6 else slice(i, S, 4)
                        for k in range(KD):
                            last = split(b[:, c * 256:(c + 1) * 256], xhi[:, k, rows], xlo[:, k, rows],
                                         w[0][:, k, :], w[1][:, k, :], k == 0, k == KD - 1)
                last.then_inc(proj_done, 1)

            for n in range(2 * N_DIL):
                proj(n)
            for s in range(SLOTS):
                n = tile_of_slot(s)
                if n is not None:
                    proj(n)
                if s == 0:
                    pe.wait_ge(proj_out, 2 * N_DIL)
                if s == DIFF0:
                    pe.wait_ge(proj_out, 2 * G_GATE)
                yt = yt_of_slot(s)
                if yt:
                    r, j = yt
                    pe.wait_ge(y_done, 4 * r + 4)
                    if 2 * r + j:
                        pe.wait_ge(yt_lo, 2 * r + j)
                    nc.tensor.transpose(bank[5][:, 0:P], yl[:, r % 2, j * P:(j + 1) * P], ident[:, :]).then_inc(yt_done, 1)
                u = s - 2
                if 0 <= u < UNITS:
                    pe.wait_ge(pT_a, u + 1)
                    if u >= 1:
                        pe.wait_ge(y_done, u)
                    if u < DIFF0:
                        pe.wait_ge(pT_b, u + 1)
                        r, h = dil(u)
                        vals = [lv[:, 0, b, h * HD:(h + 1) * HD] for b in range(4)] + \
                               [lv[:, g, r, h * HD:(h + 1) * HD] for g in (1, 2)]
                        o = bank[4][:, 0:HD]
                    else:
                        h, i = diff(u)
                        vals = [dv[:, b, h * P:(h + 1) * P] for b in range(i + 1)]
                        o = bank[4][:, 0:P]
                    for b, v in enumerate(vals):
                        last = mm(o, pT[:, u % 2, b, :], v, start=b == 0, stop=b == len(vals) - 1)
                    last.then_inc(pv_done, 1)
                u = s - 1
                if 0 <= u < UNITS:
                    if u < DIFF0:
                        pe.wait_ge(probs_done, 2 * u + 2)
                        nb = 6
                    else:
                        pe.wait_ge(comb_done, u - DIFF0 + 1)
                        nb = diff(u)[1] + 1
                    if u >= 1:
                        pe.wait_ge(pT_a, u)
                        pe.wait_ge(pT_b, min(u, DIFF0))
                    for b in range(nb):
                        o = bank[6][:, b * P:(b + 1) * P] if b < 4 else bank[7][:, (b - 4) * P:(b - 3) * P]
                        last = nc.tensor.transpose(o, sc[:, u % 2, b * P:(b + 1) * P], ident[:, :])
                    last.then_inc(tr_done, 1)
                u = s
                if u < UNITS:
                    b0, b1 = bank[2], bank[3]
                    if u >= 1:
                        pe.wait_ge(logits_done, 2 * u)
                    if u < DIFF0:
                        r, h = dil(u)
                        for g in range(3):
                            f = (4 * g + h) // 2
                            rows = slice(HD * (h % 2), HD * (h % 2) + HD)
                            if g == 0:
                                mm(b0[:, :], lq[rows, f, r::4], lk[rows, f, :], start=True, stop=True)
                            else:
                                last = mm(b1[:, (g - 1) * P:g * P], lq[rows, f, r::4], lk[rows, f, r::4], start=True, stop=True)
                    else:
                        h, i = diff(u)
                        nk = P * (i + 1)
                        for c, b in ((0, b0), (1, b1)):
                            rows = slice(HD * c, HD * c + HD)
                            last = mm(b[:, 0:nk], dq[rows, h, i * P:(i + 1) * P], dk[rows, h, 0:nk], start=True, stop=True)
                    last.then_inc(scores_done, 1)
            for n in LATE_GATES:
                proj(n)
            for h in range(HEADS):
                pe.wait_ge(norm_a, 1 + 4 * (h + 1))
                for i in range(TC):
                    last = nc.tensor.transpose(bank[2 + h][:, i * P:(i + 1) * P], yd[:, i, h * P:(h + 1) * P], ident[:, :])
                last.then_inc(yt_done, 1)
            pe.wait_ge(yt_lo, 8 + HEADS)
            pe.wait_ge(proj_out, 2 * G_BR)
            for m in range(KD):
                g = G_BR + m // 2
                pe.wait_ge(lo_done, g + 1)
                if m >= 2:
                    pe.wait_ge(prods_done, m - 1)
                w = [t[:, g % 2, 0:6 * 256].rearrange("p (k c) -> p k c", k=6) for t in (whi, wlo)]
                c = slice((m % 2) * P, (m % 2) * P + P)
                for b, hi, lo, k0, nk in ((0, yahi, yalo, 0, 4), (1, ybhi, yblo, 4, 2)):
                    for k in range(nk):
                        last = split(bank[2 * (m % 2) + b][:, :], w[0][:, k0 + k, c], w[1][:, k0 + k, c],
                                     hi[:, k, :], lo[:, k, :], k == 0, k == nk - 1)
                last.then_inc(za_done, 1)
            pe.wait_ge(prods_done, KD)
            for gi in range(N_WO):
                g = G_WO + gi
                pe.wait_ge(lo_done, g + 1)
                pe.wait_ge(mix_lo, 2 * gi + 2)
                for c in range(TC):
                    rows = slice(c * P, (c + 1) * P)
                    for j in range(2):
                        for k in range(2):
                            cols = slice(k * D + j * S, k * D + (j + 1) * S)
                            last = split(bank[2 * c + j][:, :], xhi[:, 2 * gi + k, rows], xlo[:, 2 * gi + k, rows],
                                         whi[:, g % 2, cols], wlo[:, g % 2, cols], gi == 0 and k == 0,
                                         gi == N_WO - 1 and k == 1)
                    if gi == N_WO - 1 and c < TC - 1:
                        last.then_inc(wo_done, 1)
                if gi < N_WO - 1:
                    last.then_inc(wo_group, 1)
                else:
                    last.then_inc(wo_done, 1)
            for c in range(TC):
                pe.wait_ge(ln_out, c + 1)
                for j in range(2):
                    for k in range(4):
                        last = nc.tensor.transpose(bank[2 * c + j][:, k * P:(k + 1) * P],
                                                   xn[:, c, (4 * j + k) * P:(4 * j + k + 1) * P], ident[:, :])
                    last.then_inc(xt_done, 1)

            def key_scores(n):
                pe.wait_ge(q_out, n + 1)
                if n >= 4:
                    pe.wait_ge(s_used, n - 3)
                for c in range(TC):
                    last = mm(bank[4 + n % 4][:, c * P:(c + 1) * P], qT[:, n % 2, c * P:(c + 1) * P], keys[:, n, :], start=True, stop=True)
                last.then_inc(s_done, 1)

            pe.wait_ge(xt_lo, 2 * TC)
            pe.wait_ge(keys_in, 32)
            for n in range(16):
                g = G_WQ + n // 2
                pe.wait_ge(lo_done, g + 1)
                if n >= 2:
                    pe.wait_ge(q_out, n - 1)
                w = [t[:, g % 2, :].rearrange("p (k c) -> p k c", k=KD) for t in (whi, wlo)]
                c = slice((n % 2) * P, (n % 2) * P + P)
                for k in range(KD):
                    last = split(bank[n % 2][:, :], w[0][:, k, c], w[1][:, k, c], xhi[:, k, :], xlo[:, k, :], k == 0, k == KD - 1)
                last.then_inc(q_done, 1)
                if n >= 1:
                    key_scores(n - 1)
            key_scores(15)

            def u_iteration(it, first=False, between=None):
                for s in range(2):
                    pe.wait_ge(lo_done, 2 * it + (G_U + s + 1))
                    sl = (G_U + s) % 2
                    w = [t[:, sl, :].rearrange("p (n k e) -> p n k e", n=2, k=KD) for t in (whi, wlo)]
                    for n in range(2):
                        t = 2 * s + n
                        if not first:
                            pe.wait_ge(h_gelu, 4 * it + (t - 3))
                        for k in range(KD):
                            last = split(bank[t][:, :], w[0][:, n, k, :], w[1][:, n, k, :], xhi[:, k, :], xlo[:, k, :], k == 0, k == KD - 1)
                        last.then_inc(h_done, 1)
                        if between is not None:
                            between(t)

            def transpose_picks(n):
                for c in range(TC):
                    last = nc.tensor.transpose(bank[4 + n][:, c * P:(c + 1) * P], picks[:, n, c, :], ident[:, :])
                last.then_inc(pt_done, 1)

            pe.wait_ge(q_out, 16)
            u_iteration(0, first=True)
            with pe.Fori(1, IT_A) as it:
                u_iteration(it)

            def picks_between(t):
                if t == 1:
                    pe.wait_ge(sel_done, TC)
                    transpose_picks(0)
                    transpose_picks(1)
                if t == 3:
                    pe.wait_ge(w_done, 1)
                    transpose_picks(2)

            u_iteration(IT_A, between=picks_between)
            pe.wait_ge(pt_out, 3)

            with pe.Fori(0, TC) as c:
                with pe.Fori(0, IT_G) as j:
                    def tokens(t, c=c, j=j):
                        for q in range(t * QUADS // 4, (t + 1) * QUADS // 4):
                            n = c * (P // 4) + j * QUADS + q
                            pe.wait_ge(g_free, n + 1)
                            pe.wait_ge(e_done, n + 1)
                            for k in range(4):
                                e = 4 * (q % 4) + k
                                last = mm(bank[4 + q % 4][:, k * P:(k + 1) * P], e2w[:, e, :], e1[:, e, :], start=True, stop=True)
                            last.then_inc(g_done, 1)
                    u_iteration(c * (IT_G + 1) + j + (IT_A + 1), between=tokens)
                u_iteration(c * (IT_G + 1) + (IT_G + IT_A + 1))
            for it in range(IT_A + 1 + TC * (IT_G + 1), N_U // 2):
                u_iteration(it)

            pe.wait_ge(h_gelu, NT)
            pe.wait_ge(g_free, S // 4 + 4)

            def v_iteration(it, first=False, last_it=False):
                for s in range(2):
                    pe.wait_ge(lo_done, 2 * it + (G_V + s + 1))
                    sl = (G_V + s) % 2
                    for n in range(2):
                        t = 2 * s + n
                        pe.wait_ge(a_lo, 4 * it + (t + 1))
                        end = last_it and t == 3
                        for c in range(TC):
                            rows = slice(c * P, (c + 1) * P)
                            for j in range(2):
                                cols = slice(n * D + j * S, n * D + (j + 1) * S)
                                last = split(bank[2 * c + j][:, :], ahi[:, t, rows], alo[:, t, rows],
                                             whi[:, sl, cols], wlo[:, sl, cols], first and t == 0, end)
                            if end:
                                last.then_inc(ffn_done, 1)
                        if not end:
                            last.then_inc(v_done, 1)

            v_iteration(0, first=True)
            with pe.Fori(1, N_U // 2 - 1) as it:
                v_iteration(it)
            v_iteration(N_U // 2 - 1, last_it=True)


def bucket(dist):
    n = np.maximum(dist, 0)
    nf = np.maximum(n, 1).astype(np.float32)
    large = 16 + (np.log(nf / np.float32(16)) / np.float32(math.log(2048 / 16)) * np.float32(16)).astype(np.int32)
    return np.where(n < 16, n, np.minimum(large, 31))


def bias_tiles(rel_bias):
    p = np.arange(P)[:, None]
    padded = np.concatenate([rel_bias, np.full((1, rel_bias.shape[1]), PAD, rel_bias.dtype)])

    def tile(dist, ok, heads):
        rows = np.where(ok, bucket(dist), rel_bias.shape[0])
        return np.ascontiguousarray(padded[rows][:, :, heads].transpose(0, 2, 1))

    d = p + (S - P) - np.arange(S)[None, :]
    diff = tile(d, d >= 0, slice(0, 4))
    d0 = 4 * p - (np.arange(S + 3)[None, :] - 3)
    d1 = 4 * (p - np.arange(P)[None, :])
    dil = [tile(d0, (d0 >= 0) & (d0 <= 128), slice(4, 8)), tile(d1, d1 >= 0, slice(8, 12)),
           tile(d1, (d1 >= 0) & (d1 % 16 == 0), slice(12, 16))]
    return diff, np.ascontiguousarray(np.concatenate(dil, axis=2))


def kernel(**inputs):
    import concourse.bacc as bacc
    from concourse.bass_utils import run_bass_kernel_spmd as run

    x = {k: np.asarray(v) for k, v in inputs.items()}

    def groups(w):
        n = w.shape[1] // 256
        return w.reshape(KD, P, n, 256).transpose(2, 1, 0, 3).reshape(n, P, GC)

    w_in = x["w_in"][0]
    ndq, nl = 3 * 512, 3 * 768
    w_in = np.concatenate([w_in[:, ndq:ndq + nl], w_in[:, :ndq], w_in[:, ndq + nl:]], axis=1)
    w_br = np.concatenate([x["w_branch_diff"][0], x["w_branch_dil"][0]])
    bias_d, bias_l = bias_tiles(x["rel_bias"])
    cst = np.array([STARTS[1:], np.diff(STARTS), np.arange(1, TOPK)], np.float32)
    arrays = {
        "x_t": x["x"][0].T.reshape(KD, P, S).transpose(1, 0, 2).reshape(P, KD * S),
        "x_n": x["x"][0].reshape(TC, P, D).transpose(1, 0, 2),
        "w_in": groups(w_in),
        "w_br": w_br.reshape(6, P, N_BR, 256).transpose(2, 1, 0, 3).reshape(N_BR, P, 6 * 256),
        "w_out": x["w_out"][0].reshape(KD, P, D).transpose(1, 0, 2),
        "w_q": groups(x["peer_wq"][0]),
        "keys": x["peer_keys"][0].reshape(16, P, P).transpose(2, 0, 1),
        "u": x["peer_u"][0].reshape(N_U, 2, P, KD, P).transpose(0, 4, 1, 3, 2).reshape(N_U, P, GC),
        "v": x["peer_v"][0].reshape(N_U, 2, P, D).transpose(0, 2, 1, 3).reshape(N_U, P, GC),
        "bias_d": bias_d, "bias_l": bias_l, "cst": cst,
        "diff_lambda": x["diff_lambda"].reshape(-1), "subln_g": x["diff_subln_g"].reshape(-1),
        "ln1_g": x["ln1_g"].reshape(-1), "ln1_b": x["ln1_b"].reshape(-1),
        "ln2_g": x["ln2_g"].reshape(-1), "ln2_b": x["ln2_b"].reshape(-1),
    }
    arrays = {k: np.ascontiguousarray(v) for k, v in arrays.items()}
    nc = bacc.Bacc("TRN2", target_bir_lowering=False, num_devices=1)
    aps = {k: nc.dram_tensor("in_" + k, v.shape, F32, kind="ExternalInput").ap() for k, v in arrays.items()}
    aps["out"] = nc.dram_tensor("out", [P, TC, D], F32, kind="ExternalOutput").ap()
    program(nc, aps)
    r = run(nc, [{"in_" + k: v for k, v in arrays.items()}], core_ids=[0])
    return r.results[0]["out"].transpose(1, 0, 2).reshape(1, S, D)
```

```python
import math
from contextlib import ExitStack

import numpy as np
import concourse.bass as bass
from concourse import mybir

F32 = mybir.dt.float32
F32R = mybir.dt.float32r
BF16 = mybir.dt.bfloat16
U32 = mybir.dt.uint32
ALU = mybir.AluOpType
ACT = mybir.ActivationFunctionType
AX = mybir.AxisListType.X

P = 128
S, D = 512, 1024
KD = D // P
TC = S // P
HEADS, HD = 4, 64
ALPHA = 2.0 ** 0.25
EPS = 1e-5
LAM_INIT = 0.8 - 0.6
SCALE = HD ** -0.5
PAD = -1e30
LOWEST = -3e38

GC = 2048
N_DIL, N_DIFF, N_GATE = 9, 6, 8
N_BR, N_WO, N_WQ = 4, 4, 8
G_DIFF = N_DIL
G_GATE = G_DIFF + N_DIFF
G_BR = G_GATE + N_GATE
G_WO = G_BR + N_BR
G_WQ = G_WO + N_WO
G_U = G_WQ + N_WQ
NT = 128
N_U = NT // 2
G_V = G_U + N_U

PH, TOPK = 8, 16
ROWS = [TOPK // (i + 1) for i in range(TOPK)]
CAND = sum(ROWS)
STARTS = [sum(ROWS[:i]) for i in range(TOPK)]

IT_A = 6
IT_0 = IT_A + 1
SETS, SET = 8, S // 8
IT_S = 3
QUADS = SET // 4
PIECES = 4
BW = S + 3 + 2 * P


def quads_after(tile):
    n = 4 * IT_S
    return range(-(-tile * QUADS // n), -(-(tile + 1) * QUADS // n))


class Counted:

    def __init__(self, sem):
        self.sem, self.n = sem, 0

    def by(self, ins, k=1):
        ins.then_inc(self.sem, k)
        self.n += k
        return self.n


def program(nc, a):
    es = ExitStack()
    with es:
        at = {"top": 16640}

        def place(name, shape, dt, offset):
            return nc.alloc_sbuf_tensor_at(name, shape, dt, offset=offset)

        def nbytes(shape, dt):
            return (int(np.prod(shape[1:])) * (2 if dt == BF16 else 4) + 31) // 32 * 32

        def keep(name, shape, dt=F32):
            t = place(name, shape, dt, at["top"])
            at["top"] += nbytes(shape, dt)
            return t

        class Region:

            def __init__(self, size):
                self.base, self.size = at["top"], size
                at["top"] += size
                self.at = self.base

            def phase(self, offset=0):
                self.at = self.base + offset

            def buf(self, name, shape, dt=F32):
                t = place(name, shape, dt, self.at)
                self.at += nbytes(shape, dt)
                assert self.at <= self.base + self.size, name
                return t

        xhi = keep("xhi", [P, KD, S], F32R)
        xlo = keep("xlo", [P, KD, S], F32R)
        xn = keep("xn", [P, TC, D])
        raw = keep("raw", [P, 2, GC])
        whi = keep("whi", [P, 2, GC], F32R)
        wlo = keep("wlo", [P, 2, GC], F32R)
        ident = keep("ident", [P, P])
        iota = keep("iota", [P, P])
        lam_in = keep("lam_in", [P, 4 * HD])
        lam = keep("lam", [P, 8])
        stats = keep("stats", [P, TC, 2, 6])
        mv = keep("mv", [P, TC, 2])
        rstd = keep("rstd", [P, 2, TC])
        shift = keep("shift", [P, TC])
        smax = keep("smax", [P, 2, 2])
        ssum = keep("ssum", [P, 2, 2])
        rinv = keep("rinv", [P, 2, 2])
        rneg = keep("rneg", [P, 2])
        ssq = keep("ssq", [P, 16])
        srt = keep("srt", [P, 2, 16])
        squares = keep("squares", [P, P])

        r1 = Region(49216)
        r2 = Region(32768)
        r3 = Region(24576)
        assert at["top"] <= 229344, at["top"]

        lq = r1.buf("lq", [P, 6, S])
        lk = r1.buf("lk", [P, 6, S])
        lv = r1.buf("lv", [P, 3, TC, 256])
        bias_l = r1.buf("bias_l", [P, HEADS, BW])
        dq = r2.buf("dq", [P, HEADS, S])
        dk = r2.buf("dk", [P, HEADS, S])
        dv = r2.buf("dv", [P, TC, S])
        bias_d = r2.buf("bias_d", [P, HEADS, S])
        sc = r3.buf("sc", [P, 2, 1024])
        pT = r3.buf("pT", [P, 2, 6, P])
        yl = r3.buf("yl", [P, 2, 256])
        ybhi = r3.buf("ybhi", [P, 2, S], F32R)
        yblo = r3.buf("yblo", [P, 2, S], F32R)
        r1.phase()
        gates = r1.buf("gates", [P, 16, S])
        yd = r1.buf("yd", [P, TC, S])
        subg = r1.buf("subg", [P, P])
        r2.phase()
        yahi = r2.buf("yahi", [P, HEADS, S], F32R)
        yalo = r2.buf("yalo", [P, HEADS, S], F32R)
        r3.phase()
        mixa = r3.buf("mixa", [P, 2, S])
        mixb = r3.buf("mixb", [P, 2, S])
        arena = Region(0)
        arena.base, arena.size = r1.base, r1.size + r2.size
        arena.phase()
        keys = arena.buf("keys", [P, 16, P])
        qT = arena.buf("qT", [P, 2, S])
        ln1g = arena.buf("ln1g", [P, D])
        ln1b = arena.buf("ln1b", [P, D])
        tmp128 = arena.buf("tmp128", [P, 2, P])
        val = arena.buf("val", [P, TC, 16, TOPK])
        idx = arena.buf("idx", [P, TC, 16, TOPK], U32)
        idf = arena.buf("idf", [P, 16, TOPK], BF16)
        didx = arena.buf("didx", [P, 16, TOPK - 1], BF16)
        cand = arena.buf("cand", [P, PH, CAND])
        cand2 = arena.buf("cand2", [P, PH, CAND])
        best = arena.buf("best", [P, PH, TOPK])
        bpos = arena.buf("bpos", [P, PH, TOPK], U32)
        bposf = arena.buf("bposf", [P, P], BF16)
        jf = arena.buf("jf", [P, P], BF16)
        ge = arena.buf("ge", [P, P, TOPK - 1], BF16)
        prod = arena.buf("prod", [P, P, TOPK - 1], BF16)
        sel = arena.buf("sel", [P, P])
        hsum = arena.buf("hsum", [P, 2, TC, PH])
        cst = arena.buf("cst", [P, 3, TOPK - 1])
        cstb = arena.buf("cstb", [P, 3, TOPK - 1], BF16)
        assert arena.at <= arena.base + 65536, "routing buffers lie under the stage of G"
        arena.phase()
        stage = arena.buf("stage", [P, 2 * NT, SET])
        hout = arena.buf("hout", [P, 4, S])
        picks = arena.buf("picks", [P, 3, TC, P])
        r3.phase()
        pickT = r3.buf("pickT", [P, 2, S])
        whl = r3.buf("whl", [P, S])
        whh = r3.buf("whh", [P, S], F32R)
        e1 = r3.buf("e1", [P, 8, 2, P], F32R)
        e2 = r3.buf("e2", [P, 8, P], F32R)
        arena.phase()
        hl = arena.buf("hl", [P, 2, 2, S])
        gl = arena.buf("gl", [P, 2, SETS, 2, SET])
        af = arena.buf("af", [P, 4, S])
        ahi = arena.buf("ahi", [P, 4, S], F32R)
        alo = arena.buf("alo", [P, 4, S], F32R)
        ln2g = arena.buf("ln2g", [P, D])
        ln2b = arena.buf("ln2b", [P, D])

        bank = [es.enter_context(nc.psum_tensor(f"bank{b}", [P, S], F32)) for b in range(8)]

        def g_bank(q, b):
            return bank[4 + 2 * (q % 2) + b]

        h_dram = nc.dram_tensor("h_scratch", [NT, P, S], F32, kind="Internal").ap()
        g_dram = nc.dram_tensor("g_scratch", [SETS, P, NT, SET], F32, kind="Internal").ap()

        def sem(name):
            return es.enter_context(nc.semaphore(name))

        raw_in = [sem("raw_in0"), sem("raw_in1")]
        hi_done, lo_done = sem("hi_done"), sem("lo_done")
        first_in = [sem(f"first_in{i}") for i in range(3)]
        first_hi, first_lo = sem("first_hi"), sem("first_lo")
        xt_in = [sem(f"xt_in{i}") for i in range(4)]
        x_in, x_split_hi, x_split_lo = sem("x_in"), sem("x_split_hi"), sem("x_split_lo")
        bias_in, consts_in, lam_loaded = sem("bias_in"), sem("consts_in"), sem("lam_loaded")
        id_steps, iota_done = sem("id_steps"), sem("iota_done")
        proj_done, proj_out = sem("proj_done"), sem("proj_out")
        gate_done = sem("gate_done")
        scores_done, logits_done, max_done = sem("scores_done"), sem("logits_done"), sem("max_done")
        probs_done, comb_done = sem("probs_done"), sem("comb_done")
        tr_done, pT_a, pT_b = sem("tr_done"), sem("pT_a"), sem("pT_b")
        pv_done, y_done, sq_done = sem("pv_done"), sem("y_done"), sem("sq_done")
        yt_done, yt_hi, yt_lo = sem("yt_done"), sem("yt_hi"), sem("yt_lo")
        lam_steps, lam_exp = sem("lam_steps"), sem("lam_exp")
        root_a, norm_a = sem("root_a"), sem("norm_a")
        za_done, prods_done, mix_sum, mix_hi, mix_lo = (
            sem("za_done"), sem("prods_done"), sem("mix_sum"), sem("mix_hi"), sem("mix_lo"))
        wo_group, wo_done = sem("wo_group"), sem("wo_done")
        ln_var, ln_root, ln_scaled, ln_out = sem("ln_var"), sem("ln_root"), sem("ln_scaled"), sem("ln_out")
        xt_done, xt_hi, xt_lo = sem("xt_done"), sem("xt_hi"), sem("xt_lo")
        ln_shift, ln_unit = sem("ln_shift"), sem("ln_unit")
        ln_in, keys_in = sem("ln_in"), sem("keys_in")
        q_done, q_out, s_done, s_used = sem("q_done"), sem("q_out"), sem("s_done"), sem("s_used")
        dve_step = Counted(sem("dve_step"))
        sel_done, exp_done, w_done = sem("sel_done"), sem("exp_done"), sem("w_done")
        pt_done, pt_out = sem("pt_done"), sem("pt_out")
        h_done, h_gelu = sem("h_done"), sem("h_gelu")
        h_stored = [sem(f"h_stored{i}") for i in range(4)]
        e_done, g_done, g_free, g_stored = sem("e_done"), sem("g_done"), sem("g_free"), sem("g_stored")
        hg_in = [sem("hg_in0"), sem("hg_in1")]
        a_done, a_hi, a_lo, v_done = sem("a_done"), sem("a_hi"), sem("a_lo"), sem("v_done")
        ffn_done, ln2_in, out_stored = sem("ffn_done"), sem("ln2_in"), sem("out_stored")

        block = es.enter_context(nc.Block())

        UNITS = 32
        SLOTS = UNITS + 3
        DIFF0 = 16

        GATE_SLOTS = [19, 20, 21, 23, 24, 25, 27, 28, 29, 31, 32, 33]

        def tile_of_slot(s):
            if s < 12:
                return 2 * N_DIL + s
            if s in GATE_SLOTS:
                return 2 * G_GATE + GATE_SLOTS.index(s)
            return None

        LATE_GATES = range(2 * G_GATE + 2 * N_GATE - 4, 2 * G_GATE + 2 * N_GATE)

        def dil(u):
            return u // 4, u % 4

        def diff(u):
            return (u - DIFF0) // 4, (u - DIFF0) % 4

        def yt_of_slot(s):
            for j in (0, 1):
                if (s - 6 - j) % 4 == 0 and 0 <= (s - 6 - j) // 4 < 4:
                    return (s - 6 - j) // 4, j
            return None

        def tile_kind(n):
            g = n // 2
            if 6 <= g < G_DIFF:
                return "lv"
            if G_DIFF + 4 <= g < G_GATE:
                return "dv"
            return "gate" if g >= G_GATE else "T"

        @block.sync
        def _(sp):
            def weights(g, src, cols=GC):
                if isinstance(g, int) and g >= 2 or not isinstance(g, int):
                    sp.wait_ge(lo_done, g - 1)
                return sp.dma_start(raw[:, slot_of(g), 0:cols], src)

            def slot_of(g):
                return g % 2

            for i in range(4):
                cols = slice(i * GC // 4, (i + 1) * GC // 4)
                sp.dma_start(raw[:, 0, cols], a["w_in"][0][:, cols]).then_inc(first_in[i] if i < 3 else raw_in[0], 16)
                sp.dma_start(xn[:, i, :], a["x_t"][:, i * D:(i + 1) * D]).then_inc(xt_in[i], 16)
            sp.dma_start(raw[:, 1, :], a["w_in"][1]).then_inc(raw_in[1], 16)
            for g in range(2, N_DIL):
                weights(g, a["w_in"][g]).then_inc(raw_in[g % 2], 16)
            sp.dma_start(bias_l[:, :, :], a["bias_l"]).then_inc(bias_in, 16)
            sp.dma_start(bias_d[:, :, :], a["bias_d"]).then_inc(bias_in, 16)
            sp.dma_start(lam_in[:, :], a["diff_lambda"].partition_broadcast(P)).then_inc(lam_loaded, 16)
            sp.wait_ge(x_split_lo, KD)
            sp.dma_start(xn[:, :, :], a["x_n"]).then_inc(x_in, 16)
            for g in range(N_DIL, G_BR):
                weights(g, a["w_in"][g]).then_inc(raw_in[g % 2], 16)
                if g == G_GATE + 2:
                    sp.wait_ge(y_done, DIFF0)
                    sp.dma_start(subg[:, :], a["subln_g"].partition_broadcast(P)).then_inc(consts_in, 16)
            for g in range(G_BR, G_WO):
                weights(g, a["w_br"][g - G_BR], 6 * 256).then_inc(raw_in[g % 2], 16)
            for g in range(G_WO, G_WQ):
                weights(g, a["w_out"][:, 2 * (g - G_WO):2 * (g - G_WO) + 2, :].rearrange("p k n -> p (k n)")).then_inc(raw_in[g % 2], 16)
            sp.wait_ge(mix_lo, KD)
            sp.dma_start(ln1g[:, :], a["ln1_g"].partition_broadcast(P)).then_inc(ln_in, 16)
            sp.dma_start(ln1b[:, :], a["ln1_b"].partition_broadcast(P)).then_inc(ln_in, 16)
            sp.dma_start(keys[:, :, :], a["keys"]).then_inc(keys_in, 16)
            sp.dma_start(cst[:, :, :], a["cst"].partition_broadcast(P)).then_inc(keys_in, 16)
            for g in range(G_WQ, G_U):
                weights(g, a["w_q"][g - G_WQ]).then_inc(raw_in[g % 2], 16)

            def u_load(it, s):
                sp.wait_ge(lo_done, 2 * it + (G_U + s - 1))
                sp.dma_start(raw[:, (G_U + s) % 2, :], a["u"][2 * it + s]).then_inc(raw_in[(G_U + s) % 2], 16)

            def v_load(it, s):
                sp.wait_ge(lo_done, 2 * it + (G_V + s - 1))
                sp.dma_start(raw[:, (G_V + s) % 2, :], a["v"][2 * it + s]).then_inc(raw_in[(G_V + s) % 2], 16)

            def h_store(it, t):
                sp.wait_ge(h_gelu, 4 * it + (t + 1))
                sp.dma_start(h_dram[4 * it + t], hout[:, t, :]).then_inc(h_stored[t], 16)

            def g_piece(n, half, i):
                k = i * (NT // PIECES)
                sp.dma_start(g_dram[n][:, k:k + NT // PIECES, :],
                             stage[:, bass.ds(half * NT + k, NT // PIECES), :]).then_inc(g_stored, 16)

            def u_iteration(it, piece=None):
                for s in range(2):
                    u_load(it + 1, s)
                    h_store(it, 2 * s)
                    h_store(it, 2 * s + 1)
                    if piece is not None:
                        piece(s)

            u_load(0, 0)
            u_load(0, 1)
            with sp.Fori(0, IT_0 + IT_S) as it:
                u_iteration(it)
            with sp.Fori(1, SETS) as n:
                sp.wait_ge(g_free, n * QUADS + 2)
                for k in range(IT_S):
                    def piece(s, n=n, k=k):
                        if 2 * k + s < PIECES:
                            g_piece(n - 1, (n + 1) % 2, 2 * k + s)
                    u_iteration(n * IT_S + (IT_0 + k), piece)

            def hg_load(it, s):
                n = 4 * it + 2 * s
                sp.dma_start(hl[:, s, :, :], h_dram[bass.ds(n, 2)].rearrange("n m t -> m n t")).then_inc(hg_in[s], 16)
                sp.dma_start(gl[:, s, :, :, :], g_dram[:, :, bass.ds(n, 2), :].rearrange("s m n t -> m s n t")).then_inc(hg_in[s], 16)

            assert IT_0 + SETS * IT_S == N_U // 2 - 1
            sp.wait_ge(g_free, SETS * QUADS + 2)
            for i in range(PIECES):
                g_piece(SETS - 1, (SETS - 1) % 2, i)
            v_load(0, 0)
            h_store(N_U // 2 - 1, 0)
            h_store(N_U // 2 - 1, 1)
            for t in range(4):
                sp.wait_ge(h_stored[t], 16)
            sp.wait_ge(g_stored, 16 * PIECES * SETS)
            hg_load(0, 0)
            hg_load(0, 1)
            v_load(0, 1)
            h_store(N_U // 2 - 1, 2)
            h_store(N_U // 2 - 1, 3)
            for t in range(4):
                sp.wait_ge(h_stored[t], 16 * (NT // 4))
            sp.dma_start(ln2g[:, :], a["ln2_g"].partition_broadcast(P)).then_inc(ln2_in, 16)
            sp.dma_start(ln2b[:, :], a["ln2_b"].partition_broadcast(P)).then_inc(ln2_in, 16)
            with sp.Fori(0, N_U // 2 - 1) as it:
                for s in range(2):
                    v_load(it + 1, s)
                    sp.wait_ge(a_done, 4 * it + (2 * s + 2))
                    hg_load(it + 1, s)
            for c in range(TC):
                for j in range(2):
                    cols = slice(j * S, (j + 1) * S)
                    sp.wait_ge(ln_out, TC + 2 * c + (j + 1))
                    sp.dma_start(a["out"][:, c, cols], xn[:, c, cols]).then_inc(out_stored, 16)
            sp.wait_ge(out_stored, 32 * TC)

        @block.gpsimd
        def _(pool):
            nc.gpsimd.memset(ident[:, :], 0.0).then_inc(id_steps, 1)
            nc.gpsimd.iota(iota[:, :], [[1, P]], base=0, channel_multiplier=0,
                           allow_small_or_imprecise_dtypes=True).then_inc(iota_done, 1)
            pool.wait_ge(id_steps, 1)
            nc.gpsimd.affine_select(out=ident[:, :], in_=ident[:, :], compare_op=ALU.not_equal, fill=1.0,
                                    base=0, pattern=[[-1, P]], channel_multiplier=1).then_inc(id_steps, 1)

            def low(g, cols=GC):
                pool.wait_ge(hi_done, g + 1)
                s = g % 2
                nc.gpsimd.tensor_tensor(wlo[:, s, 0:cols], raw[:, s, 0:cols],
                                        whi[:, s, 0:cols].bitcast(F32), ALU.subtract).then_inc(lo_done, 1)

            for i in range(4):
                cols = slice(i * GC // 4, (i + 1) * GC // 4)
                if i < 3:
                    pool.wait_ge(first_hi, i + 1)
                else:
                    pool.wait_ge(hi_done, 1)
                nc.gpsimd.tensor_tensor(wlo[:, 0, cols], raw[:, 0, cols], whi[:, 0, cols].bitcast(F32),
                                        ALU.subtract).then_inc(first_lo if i < 3 else lo_done, 1)
            low(1)
            for g in range(2, G_BR):
                low(g)
            low(G_BR, 6 * 256)
            low(G_BR + 1, 6 * 256)
            for m in range(KD):
                if m % 2 == 0 and m >= 2:
                    low(G_BR + m // 2 + 1, 6 * 256 if m // 2 + 1 < N_BR else GC)
                pool.wait_ge(mix_hi, m + 1)
                nc.gpsimd.tensor_tensor(xlo[:, m, :], mixa[:, m % 2, :], xhi[:, m, :].bitcast(F32), ALU.subtract).then_inc(mix_lo, 1)
            for g in range(G_WO + 1, G_WQ):
                low(g)
            pool.wait_ge(ln_in, 32)
            for c in range(TC):
                pool.wait_ge(ln_scaled, c + 1)
                nc.gpsimd.tensor_tensor(xn[:, c, :], xn[:, c, :], ln1b[:, :], ALU.add).then_inc(ln_out, 1)
            for g in range(G_WQ, G_U):
                low(g)

            with pool.Fori(0, N_U) as it:
                for s in range(2):
                    pool.wait_ge(hi_done, 2 * it + (G_U + s + 1))
                    sl = (G_U + s) % 2
                    nc.gpsimd.tensor_tensor(wlo[:, sl, :], raw[:, sl, :],
                                            whi[:, sl, :].bitcast(F32), ALU.subtract).then_inc(lo_done, 1)
            pool.wait_ge(ln2_in, 32)
            for c in range(TC):
                for j in range(2):
                    cols = slice(j * S, (j + 1) * S)
                    pool.wait_ge(ln_scaled, TC + 2 * c + (j + 1))
                    nc.gpsimd.tensor_tensor(xn[:, c, cols], xn[:, c, cols], ln2b[:, cols], ALU.add).then_inc(ln_out, 1)

        @block.scalar
        def _(act):
            def high(g, cols=GC):
                s = g % 2
                act.wait_ge(raw_in[s], 16 * (g // 2 + 1))
                nc.scalar.activation(whi[:, s, 0:cols], raw[:, s, 0:cols], ACT.Copy).then_inc(hi_done, 1)

            xt = xn[:, :, :].rearrange("p a b -> p (a b)").rearrange("p (k t) -> p k t", k=KD)
            for k in range(KD):
                if k % 2 == 0:
                    i = k // 2
                    cols = slice(i * GC // 4, (i + 1) * GC // 4)
                    act.wait_ge(first_in[i] if i < 3 else raw_in[0], 16)
                    nc.scalar.activation(whi[:, 0, cols], raw[:, 0, cols], ACT.Copy).then_inc(first_hi if i < 3 else hi_done, 1)
                    act.wait_ge(xt_in[i], 16)
                nc.scalar.activation(xhi[:, k, :], xt[:, k, :], ACT.Copy).then_inc(x_split_hi, 1)
            high(1)

            def proj_evac(n):
                act.wait_ge(proj_done, n + 1)
                g, half, b = n // 2, n % 2, bank[n % 2]
                kind = tile_kind(n)
                if kind == "T":
                    if g < G_DIFF:
                        dst = (lq if g < 3 else lk)[:, n % 6, :]
                    else:
                        m = n - 2 * G_DIFF
                        dst = (dq if m < 4 else dk)[:, m % 4, :]
                    nc.scalar.activation(dst, b[:, :], ACT.Copy).then_inc(proj_out, 1)
                elif kind == "lv":
                    nc.scalar.activation(lv[:, g - 6, 2 * half:2 * half + 2, :],
                                         b[:, :].rearrange("p (c n) -> p c n", c=2), ACT.Copy).then_inc(proj_out, 1)
                elif kind == "dv":
                    col = 256 * (g - G_DIFF - 4)
                    nc.scalar.activation(dv[:, 2 * half:2 * half + 2, col:col + 256],
                                         b[:, :].rearrange("p (c n) -> p c n", c=2), ACT.Copy).then_inc(proj_out, 1)
                else:
                    nc.scalar.activation(gates[:, n - 2 * G_GATE, :], b[:, :],
                                         ACT.Sigmoid if n in LATE_GATES else ACT.Copy).then_inc(proj_out, 1)
                if half == 1:
                    high_next(g + 2)

            def high_next(g):
                if g < G_BR:
                    high(g)
                elif g < G_WO:
                    high(g, 6 * 256)

            for n in range(2 * N_DIL):
                proj_evac(n)
            act.wait_ge(lam_steps, 2)
            nc.scalar.activation(lam[:, 2:4], lam[:, 0:2], ACT.Exp).then_inc(lam_exp, 1)

            for s in range(SLOTS):
                n = tile_of_slot(s)
                if n is not None:
                    proj_evac(n)
                yt = yt_of_slot(s)
                if yt:
                    r, j = yt
                    act.wait_ge(yt_done, 2 * r + j + 1)
                    nc.scalar.activation(ybhi[:, j, r::4], bank[5][:, 0:P], ACT.Copy).then_inc(yt_hi, 1)
                u = s - 2
                if DIFF0 <= u < UNITS:
                    h, i = diff(u)
                    act.wait_ge(y_done, u + 1)
                    act.wait_ge(pv_done, u + 1)
                    nc.scalar.activation(squares[:, :], yd[:, i, h * P:h * P + P], ACT.Square,
                                         accum_out=ssq[:, u - DIFF0:u - DIFF0 + 1]).then_inc(sq_done, 1)
                u = s - 1
                if 0 <= u < UNITS:
                    act.wait_ge(tr_done, u + 1)
                    if u >= 2:
                        act.wait_ge(pv_done, u - 1)
                    nb = 4 if u < DIFF0 else diff(u)[1] + 1
                    nc.scalar.activation(pT[:, u % 2, 0:nb, :], bank[6][:, 0:nb * P].rearrange("p (b q) -> p b q", b=nb), ACT.Copy).then_inc(pT_a, 1)
                u = s
                if u < UNITS:
                    act.wait_ge(max_done, u + 1)
                    if u >= 2:
                        act.wait_ge(y_done, u - 1)
                    if u < DIFF0:
                        nc.scalar.activation(sc[:, u % 2, 0:768], sc[:, u % 2, 0:768], ACT.Exp, bias=smax[:, u % 2, 0:1],
                                             accum_out=ssum[:, u % 2, 0:1]).then_inc(probs_done, 2)
                    else:
                        nk = P * (diff(u)[1] + 1)
                        for c in range(2):
                            v = sc[:, u % 2, c * S:c * S + nk]
                            nc.scalar.activation(v, v, ACT.Exp, bias=smax[:, u % 2, c:c + 1],
                                                 accum_out=ssum[:, u % 2, c:c + 1]).then_inc(probs_done, 1)
            act.wait_ge(norm_a, 1)
            nc.scalar.activation(srt[:, 1, :], srt[:, 0, :], ACT.Sqrt).then_inc(root_a, 1)
            for i in range(3):
                if i < 2:
                    proj_evac(LATE_GATES[i])
                act.wait_ge(proj_out, LATE_GATES[0])
                nc.scalar.activation(gates[:, 4 * i:4 * i + 4, :], gates[:, 4 * i:4 * i + 4, :], ACT.Sigmoid).then_inc(gate_done, 1)
            for h in range(HEADS):
                act.wait_ge(yt_done, 8 + h + 1)
                nc.scalar.activation(yahi[:, h, :], bank[2 + h][:, :], ACT.Copy).then_inc(yt_hi, 1)
            for n in LATE_GATES[2:]:
                proj_evac(n)
            for m in range(KD):
                act.wait_ge(mix_sum, m + 1)
                nc.scalar.activation(xhi[:, m, :], mixa[:, m % 2, :], ACT.Copy).then_inc(mix_hi, 1)
                if m % 2 == 1 and m // 2 < 3:
                    g = G_BR + m // 2 + 2
                    act.wait_ge(za_done, m + 1)
                    high(g, 6 * 256 if g < G_WO else GC)
            act.wait_ge(za_done, KD)
            high(G_WO + 1)
            for g in range(G_WO + 2, G_WQ):
                act.wait_ge(wo_group, g - G_WO - 1)
                high(g)

            def layer_norm(base, parts=1, before_last=None):
                for c in range(TC):
                    if c == TC - 1 and before_last:
                        before_last()
                    act.wait_ge(ln_var, base + c + 1)
                    nc.scalar.activation(rstd[:, 0, c:c + 1], mv[:, c, 1:2], ACT.Sqrt).then_inc(ln_root, 1)
                    act.wait_ge(ln_shift, base + c + 1)
                    for j in range(parts):
                        o = xn[:, c, j * D // parts:(j + 1) * D // parts]
                        nc.scalar.activation(o, o, ACT.Identity, bias=shift[:, c:c + 1],
                                             scale=rstd[:, 1, c:c + 1]).then_inc(ln_unit, 1)

            def first_query_weights():
                act.wait_ge(wo_done, TC)
                high(G_WQ)

            layer_norm(0, before_last=first_query_weights)
            high(G_WQ + 1)
            for c in range(TC):
                for j in range(2):
                    act.wait_ge(xt_done, 2 * c + j + 1)
                    nc.scalar.activation(xhi[:, 4 * j:4 * j + 4, c * P:c * P + P],
                                         bank[2 * c + j][:, :].rearrange("p (k t) -> p k t", k=4), ACT.Copy).then_inc(xt_hi, 1)
            for n in range(16):
                act.wait_ge(q_done, n + 1)
                if n >= 2:
                    act.wait_ge(s_done, n - 1)
                nc.scalar.activation(qT[:, n % 2, :], bank[n % 2][:, :], ACT.Copy).then_inc(q_out, 1)
                if n % 2 == 1:
                    high(G_WQ + n // 2 + 2)

            def gelu(it, t, stored):
                act.wait_ge(h_done, 4 * it + (t + 1))
                if stored:
                    act.wait_ge(h_stored[t], 16 * it)
                nc.scalar.activation(hout[:, t, :], bank[t][:, :], ACT.Gelu).then_inc(h_gelu, 1)

            def high_it(it, s, base):
                sl = (base + s) % 2
                act.wait_ge(raw_in[sl], 16 * it + 16 * ((base + s) // 2 + 1))
                nc.scalar.activation(whi[:, sl, :], raw[:, sl, :], ACT.Copy).then_inc(hi_done, 1)

            def u_iteration(it, stored=True, quads=None, between=None):
                for s in range(2):
                    for t in (2 * s, 2 * s + 1):
                        gelu(it, t, stored)
                        if quads is not None:
                            quads(t)
                    high_it(it, s, G_U + 2)
                    if between is not None and s == 0:
                        between()

            u_iteration(0, stored=False)
            with act.Fori(1, IT_A) as it:
                u_iteration(it)
            act.wait_ge(sel_done, TC)
            nc.scalar.activation(picks[:, 2, :, :], picks[:, 2, :, :], ACT.Exp).then_inc(exp_done, 1)
            u_iteration(IT_A)
            with act.Fori(IT_0, N_U // 2 - 1) as it:
                u_iteration(it)

            def high_a(it, t):
                act.wait_ge(a_done, 4 * it + (t + 1))
                nc.scalar.activation(ahi[:, t, :], af[:, t, :], ACT.Copy).then_inc(a_hi, 1)

            def first_high_a():
                high_a(0, 0)
                high_a(0, 1)

            u_iteration(N_U // 2 - 1, between=first_high_a)
            with act.Fori(0, N_U // 2 - 1) as it:
                high_a(it, 2)
                high_a(it, 3)
                act.wait_ge(v_done, 4 * it + 2)
                high_it(it, 0, G_V + 2)
                high_a(it + 1, 0)
                high_a(it + 1, 1)
                act.wait_ge(v_done, 4 * it + 4)
                high_it(it, 1, G_V + 2)
            high_a(N_U // 2 - 1, 2)
            high_a(N_U // 2 - 1, 3)
            layer_norm(TC, parts=2)

        @block.vector
        def _(dve):
            V = nc.vector

            def step(ins):
                dve.wait_ge(dve_step.sem, dve_step.by(ins))

            xt = xn[:, :, :].rearrange("p a b -> p (a b)").rearrange("p (k t) -> p k t", k=KD)
            for k in range(KD):
                dve.wait_ge(x_split_hi, k + 1)
                V.tensor_tensor(xlo[:, k, :], xt[:, k, :], xhi[:, k, :].bitcast(F32), ALU.subtract).then_inc(x_split_lo, 1)
            dve.wait_ge(lam_loaded, 16)
            for j in range(2):
                v = lam_in[:, 2 * j * HD:(2 * j + 2) * HD].rearrange("p (a d) -> p a d", a=2)
                V.tensor_tensor_reduce(out=v[:, 0, :], in0=v[:, 0, :], in1=v[:, 1, :], scale=1.0, scalar=0.0,
                                       op0=ALU.mult, op1=ALU.add, accum_out=lam[:, j:j + 1]).then_inc(lam_steps, 1)
            dve.wait_ge(lam_exp, 1)
            step(V.tensor_tensor(lam[:, 4:5], lam[:, 3:4], lam[:, 2:3], ALU.subtract))
            step(V.tensor_scalar(lam[:, 4:5], lam[:, 4:5], -LAM_INIT, None, ALU.add))
            dve.wait_ge(bias_in, 32)

            for s in range(SLOTS):
                u = s - 1
                if DIFF0 <= u < UNITS:
                    h, i = diff(u)
                    w, nk = u % 2, P * (i + 1)
                    dve.wait_ge(probs_done, 2 * u + 2)
                    step(V.reciprocal(rinv[:, w, :], ssum[:, w, :]))
                    step(V.tensor_tensor(rneg[:, w:w + 1], rinv[:, w, 1:2], lam[:, 4:5], ALU.mult))
                    step(V.tensor_scalar(sc[:, w, 0:nk], sc[:, w, 0:nk], rinv[:, w, 0:1], None, ALU.mult))
                    V.scalar_tensor_tensor(sc[:, w, 0:nk], sc[:, w, S:S + nk], rneg[:, w:w + 1], sc[:, w, 0:nk],
                                           ALU.mult, ALU.add).then_inc(comb_done, 1)
                u = s
                if u < UNITS:
                    w = u % 2
                    b0, b1 = bank[2], bank[3]
                    dve.wait_ge(scores_done, u + 1)
                    if u >= 2:
                        dve.wait_ge(tr_done, u - 1)
                    if u < DIFF0:
                        r, h = dil(u)
                        V.scalar_tensor_tensor(sc[:, w, 0:S], b0[:, :], SCALE, bias_l[:, h, 3 - r:3 - r + S], ALU.mult, ALU.add).then_inc(logits_done, 1)
                        V.scalar_tensor_tensor(sc[:, w, S:S + 2 * P], b1[:, 0:2 * P], SCALE, bias_l[:, h, S + 3:BW], ALU.mult, ALU.add).then_inc(logits_done, 1)
                        dve.wait_ge(logits_done, 2 * u + 2)
                        V.tensor_reduce(smax[:, w, 0:1], sc[:, w, 0:768], AX, ALU.max, negate=True).then_inc(max_done, 1)
                    else:
                        h, i = diff(u)
                        nk = P * (i + 1)
                        for c, b in ((0, b0), (1, b1)):
                            V.scalar_tensor_tensor(sc[:, w, c * S:c * S + nk], b[:, 0:nk], SCALE,
                                                   bias_d[:, h, S - nk:S], ALU.mult, ALU.add).then_inc(logits_done, 1)
                        dve.wait_ge(logits_done, 2 * u + 2)
                        V.tensor_reduce(smax[:, w, :], sc[:, w, :].rearrange("p (c k) -> p c k", c=2)[:, :, 0:nk], AX, ALU.max, negate=True).then_inc(max_done, 1)
                yt = yt_of_slot(s)
                if yt:
                    r, j = yt
                    dve.wait_ge(yt_hi, 2 * r + j + 1)
                    V.tensor_tensor(yblo[:, j, r::4], bank[5][:, 0:P], ybhi[:, j, r::4].bitcast(F32), ALU.subtract).then_inc(yt_lo, 1)
                u = s - 2
                if 0 <= u < UNITS:
                    dve.wait_ge(pv_done, u + 1)
                    if u < DIFF0:
                        r, h = dil(u)
                        if r >= 2 and h == 0:
                            dve.wait_ge(yt_done, 2 * (r - 1))
                        step(V.reciprocal(rinv[:, u % 2, 0:1], ssum[:, u % 2, 0:1]))
                        V.tensor_scalar(yl[:, r % 2, h * HD:(h + 1) * HD], bank[4][:, 0:HD],
                                        rinv[:, u % 2, 0:1], None, ALU.mult).then_inc(y_done, 1)
                    else:
                        h, i = diff(u)
                        V.tensor_copy(yd[:, i, h * P:(h + 1) * P], bank[4][:, 0:P]).then_inc(y_done, 1)
                u = s - 1
                if 0 <= u < DIFF0:
                    dve.wait_ge(tr_done, u + 1)
                    if u >= 2:
                        dve.wait_ge(pv_done, u - 1)
                    V.tensor_copy(pT[:, u % 2, 4:6, :], bank[7][:, 0:256].rearrange("p (b q) -> p b q", b=2)).then_inc(pT_b, 1)

            dve.wait_ge(sq_done, 16)
            V.tensor_scalar(srt[:, 0, :], ssq[:, :], 1.0 / P, EPS, ALU.mult, ALU.add).then_inc(norm_a, 1)
            dve.wait_ge(consts_in, 16)
            step(V.tensor_scalar(subg[:, :], subg[:, :], 1.0 - LAM_INIT, None, ALU.mult))
            dve.wait_ge(root_a, 1)
            step(V.reciprocal(srt[:, 0, :], srt[:, 1, :]))
            for h in range(HEADS):
                for i in range(TC):
                    o = yd[:, i, h * P:(h + 1) * P]
                    k = 4 * h + i
                    V.scalar_tensor_tensor(o, o, srt[:, 0, k:k + 1], subg[:, :], ALU.mult, ALU.mult).then_inc(norm_a, 1)
            for h in range(HEADS):
                dve.wait_ge(yt_hi, 8 + h + 1)
                V.tensor_tensor(yalo[:, h, :], bank[2 + h][:, :], yahi[:, h, :].bitcast(F32), ALU.subtract).then_inc(yt_lo, 1)

            for m in range(KD):
                dve.wait_ge(za_done, m + 1)
                if m == 0:
                    dve.wait_ge(gate_done, 3)
                if m >= 4:
                    dve.wait_ge(proj_out, 2 * G_GATE + KD + m + 1)
                if m >= 2:
                    dve.wait_ge(mix_lo, m - 1)
                b0, b1 = bank[2 * (m % 2)], bank[2 * (m % 2) + 1]
                V.tensor_tensor(mixa[:, m % 2, :], b0[:, :], gates[:, m, :], ALU.mult)
                V.tensor_tensor(mixb[:, m % 2, :], b1[:, :], gates[:, KD + m, :], ALU.mult).then_inc(prods_done, 1)
                dve.wait_ge(prods_done, m + 1)
                V.tensor_tensor(mixa[:, m % 2, :], mixa[:, m % 2, :], mixb[:, m % 2, :], ALU.add).then_inc(mix_sum, 1)

            def norm_first(c, b, done, n):
                dve.wait_ge(done, n)
                for j in range(2):
                    o = xn[:, c, j * S:(j + 1) * S]
                    k = dve_step.by(V.scalar_tensor_tensor(o, o, ALPHA, b[j][:, :], ALU.mult, ALU.add))
                dve.wait_ge(dve_step.sem, k)
                for j in range(2):
                    k = dve_step.by(V.bn_stats(stats[:, c, j, :], xn[:, c, j * S:(j + 1) * S]))
                dve.wait_ge(dve_step.sem, k)
                step(V.bn_aggr(mv[:, c, :], stats[:, c, :, :].rearrange("p a b -> p (a b)")))
                V.tensor_scalar(mv[:, c, 1:2], mv[:, c, 1:2], EPS, None, ALU.add).then_inc(ln_var, 1)

            def norm_rest(c, base, gamma, parts=1):
                for j in range(parts):
                    cols = slice(j * D // parts, (j + 1) * D // parts)
                    dve.wait_ge(ln_unit, base + parts * c + (j + 1))
                    V.tensor_tensor(xn[:, c, cols], xn[:, c, cols], gamma[:, cols], ALU.mult).then_inc(ln_scaled, 1)

            def norm_shift(c, base):
                dve.wait_ge(ln_root, base + c + 1)
                step(V.reciprocal(rstd[:, 1, c:c + 1], rstd[:, 0, c:c + 1]))
                V.scalar_tensor_tensor(shift[:, c:c + 1], mv[:, c, 0:1], -1.0, rstd[:, 1, c:c + 1], ALU.mult, ALU.mult).then_inc(ln_shift, 1)

            dve.wait_ge(x_in, 16)
            dve.wait_ge(ln_in, 32)
            for c in range(TC + 1):
                if c < TC:
                    norm_first(c, (bank[2 * c], bank[2 * c + 1]), wo_done, c + 1)
                if c >= 1:
                    norm_rest(c - 1, 0, ln1g)
                if c < TC:
                    norm_shift(c, 0)
            for c in range(TC):
                for j in range(2):
                    dve.wait_ge(xt_hi, 2 * c + j + 1)
                    o = (slice(None), slice(4 * j, 4 * j + 4), slice(c * P, c * P + P))
                    V.tensor_tensor(xlo[o], bank[2 * c + j][:, :].rearrange("p (k t) -> p k t", k=4),
                                    xhi[o].bitcast(F32), ALU.subtract).then_inc(xt_lo, 1)

            dve.wait_ge(keys_in, 32)
            step(V.tensor_copy(cstb[:, :, :], cst[:, :, :]))
            for n in range(16):
                dve.wait_ge(s_done, n + 1)
                b = bank[4 + n % 4]
                for c in range(TC):
                    sco = b[:, c * P:(c + 1) * P]
                    v, x, t = val[:, c, n, :], idx[:, c, n, :], tmp128[:, c % 2, :]
                    step(V.max(v[:, 0:8], sco))
                    V.max_index(x[:, 0:8], v[:, 0:8], sco)
                    k = V.match_replace(t, v[:, 0:8], sco, LOWEST)
                    if c == TC - 1:
                        k.then_inc(s_used, 1)
                        dve.wait_ge(s_used, n + 1)
                    else:
                        dve.wait_ge(dve_step.sem, dve_step.by(k))
                    step(V.max(v[:, 8:16], t))
                    step(V.max_index(x[:, 8:16], v[:, 8:16], t))
            for c in range(TC):
                vv = val[:, c, :, :].rearrange("p (h c) k -> p h c k", c=2)
                step(V.tensor_copy(idf[:, :, :], idx[:, c, :, :]))
                step(V.tensor_tensor(didx[:, :, :], idf[:, :, 1:TOPK], idf[:, :, 0:TOPK - 1], ALU.subtract))
                i = 0
                while i < TOPK:
                    w = ROWS[i]
                    rows = len([x for x in ROWS if x == w])
                    o = cand[:, :, STARTS[i]:STARTS[i] + rows * w].rearrange("p h (i j) -> p h i j", j=w)
                    v1 = vv[:, :, 0, i:i + rows].unsqueeze(3).to_broadcast([P, PH, rows, w])
                    v2 = vv[:, :, 1, 0:w].unsqueeze(2).to_broadcast([P, PH, rows, w])
                    k = dve_step.by(V.tensor_tensor(o, v1, v2, ALU.add))
                    i += rows
                dve.wait_ge(dve_step.sem, k)
                for h in range(PH):
                    k = dve_step.by(V.max(best[:, h, 0:8], cand[:, h, :]))
                dve.wait_ge(dve_step.sem, k)
                for h in range(PH):
                    V.max_index(bpos[:, h, 0:8], best[:, h, 0:8], cand[:, h, :])
                    k = dve_step.by(V.match_replace(cand2[:, h, :], best[:, h, 0:8], cand[:, h, :], LOWEST))
                dve.wait_ge(dve_step.sem, k)
                for h in range(PH):
                    k = dve_step.by(V.max(best[:, h, 8:16], cand2[:, h, :]))
                dve.wait_ge(dve_step.sem, k)
                for h in range(PH):
                    k = dve_step.by(V.max_index(bpos[:, h, 8:16], best[:, h, 8:16], cand2[:, h, :]))
                dve.wait_ge(dve_step.sem, k)
                step(V.tensor_copy(bposf[:, :], bpos[:, :, :].rearrange("p h k -> p (h k)")))
                NR = TOPK - 1

                def row_of(n):
                    return cstb[:, n, :].unsqueeze(1).to_broadcast([P, P, NR])

                def by_head(half):
                    return (didx[:, :, :].rearrange("p (h c) k -> p h c k", c=2)[:, :, half, :]
                            .unsqueeze(2).to_broadcast([P, PH, TOPK, NR]))

                def heads(t):
                    return t[:, :, :].rearrange("p (h s) k -> p h s k", h=PH)

                def first_key(half):
                    return (idf[:, :, :].rearrange("p (h c) k -> p h c k", c=2)[:, :, half, 0]
                            .unsqueeze(2).to_broadcast([P, PH, TOPK]))

                def pick(n):
                    return picks[:, n, c, :].rearrange("p (h s) -> p h s", h=PH)

                step(V.tensor_tensor(ge[:, :, :], bposf[:, :].unsqueeze(2).to_broadcast([P, P, NR]), row_of(0), ALU.is_ge))
                step(V.tensor_tensor(heads(prod), heads(ge), by_head(0), ALU.mult))
                step(V.tensor_reduce(sel[:, :], prod[:, :, :], AX, ALU.add))
                step(V.tensor_tensor(pick(0), sel[:, :].rearrange("p (h s) -> p h s", h=PH), first_key(0), ALU.add))
                step(V.tensor_tensor(prod[:, :, :], ge[:, :, :], row_of(1), ALU.mult))
                step(V.tensor_reduce(sel[:, :], prod[:, :, :], AX, ALU.add))
                step(V.tensor_tensor(jf[:, :], bposf[:, :], sel[:, :], ALU.subtract))
                step(V.tensor_tensor(ge[:, :, :], jf[:, :].unsqueeze(2).to_broadcast([P, P, NR]), row_of(2), ALU.is_ge))
                step(V.tensor_tensor(heads(prod), heads(ge), by_head(1), ALU.mult))
                step(V.tensor_reduce(sel[:, :], prod[:, :, :], AX, ALU.add))
                V.tensor_tensor(pick(1), sel[:, :].rearrange("p (h s) -> p h s", h=PH), first_key(1), ALU.add)
                V.tensor_tensor(pick(2), best[:, :, :], best[:, :, 0:1].to_broadcast([P, PH, TOPK]), ALU.subtract).then_inc(sel_done, 1)
                dve.wait_ge(sel_done, c + 1)
            dve.wait_ge(exp_done, 1)
            w4 = picks[:, 2, :, :].rearrange("p c (h s) -> p (c h) s", h=PH)
            hs = [hsum[:, j, :, :].rearrange("p c h -> p (c h)") for j in range(2)]
            step(V.tensor_reduce(hs[0], w4, AX, ALU.add))
            step(V.reciprocal(hs[1], hs[0]))
            V.tensor_tensor(w4, w4, hs[1].unsqueeze(2).to_broadcast([P, TC * PH, TOPK]), ALU.mult).then_inc(w_done, 1)
            for n in range(3):
                dve.wait_ge(pt_done, n + 1)
                if n < 2:
                    V.tensor_copy(pickT[:, n, :], bank[4 + n][:, :]).then_inc(pt_out, 1)
            step(V.tensor_copy(whh[:, :], bank[6][:, :]))
            V.tensor_tensor(whl[:, :], bank[6][:, :], whh[:, :].bitcast(F32), ALU.subtract).then_inc(pt_out, 1)
            dve.wait_ge(pt_out, 3)
            dve.sem_inc(g_free, 2)

            def one_hots(n, q, used=True):
                if used:
                    dve.wait_ge(g_done, n * QUADS + (q - 1))
                for k in range(4):
                    e = 4 * (q % 2) + k
                    t = bass.ds(n * SET + (4 * q + k), 1)
                    V.tensor_scalar(e2[:, e, :], iota[:, :], pickT[:, 1, t], None, ALU.is_equal)
                    V.tensor_scalar(e1[:, e, 0, :], iota[:, :], pickT[:, 0, t], whh[:, t].bitcast(F32), ALU.is_equal, ALU.mult)
                    last = V.tensor_scalar(e1[:, e, 1, :], iota[:, :], pickT[:, 0, t], whl[:, t], ALU.is_equal, ALU.mult)
                last.then_inc(e_done, 1)

            def build_set(n, half, first=False, last=False):
                for q in range(QUADS):
                    if not (last and q == QUADS - 1):
                        one_hots(n, q + 1, used=not (first and q == 0))
                    dve.wait_ge(g_done, n * QUADS + (q + 1))
                    for b in range(2):
                        parts = g_bank(q, b)[:, :].rearrange("p (t a n) -> p t n a", t=2, a=2)
                        o = stage[:, bass.ds(half * NT, NT), 4 * q + 2 * b:4 * q + 2 * b + 2].rearrange("p n t -> p t n")
                        k = V.tensor_reduce(o, parts, AX, ALU.add)
                    k.then_inc(g_free, 1)

            one_hots(0, 0, used=False)
            build_set(0, 0, first=True)
            with dve.Fori(1, SETS - 1) as n:
                build_set(n, n % 2)
                dve.wait_ge(g_stored, n * (16 * PIECES))
            build_set(SETS - 1, (SETS - 1) % 2, last=True)

            def v_iteration(it, first=False):
                for s in range(2):
                    dve.wait_ge(hg_in[s], 32 * it + 32)
                    for t in (2 * s, 2 * s + 1):
                        if not first:
                            dve.wait_ge(a_lo, 4 * it + (t - 3))
                        V.tensor_tensor(af[:, t, :].rearrange("p (s t) -> p s t", s=SETS),
                                        hl[:, s, t % 2, :].rearrange("p (s t) -> p s t", s=SETS),
                                        gl[:, s, :, t % 2, :], ALU.mult).then_inc(a_done, 1)
                    for t in (2 * s, 2 * s + 1):
                        dve.wait_ge(a_hi, 4 * it + (t + 1))
                        V.tensor_tensor(alo[:, t, :], af[:, t, :], ahi[:, t, :].bitcast(F32), ALU.subtract).then_inc(a_lo, 1)

            v_iteration(0, first=True)
            with dve.Fori(1, N_U // 2) as it:
                v_iteration(it)
            dve.wait_ge(ln2_in, 32)
            for c in range(TC + 1):
                if c < TC:
                    norm_first(c, (bank[2 * c], bank[2 * c + 1]), ffn_done, c + 1)
                if c >= 1:
                    norm_rest(c - 1, TC, ln2g, parts=2)
                if c < TC:
                    norm_shift(c, TC)

        @block.tensor
        def _(pe):
            mm = nc.tensor.matmul

            def split(out, lh, ll, rh, rl, first, last):
                mm(out, lh, rh, start=first, stop=False)
                mm(out, lh, rl, start=False, stop=False)
                return mm(out, ll, rh, start=False, stop=last)

            pe.wait_ge(id_steps, 2)

            def proj(n):
                g, half, b = n // 2, n % 2, bank[n % 2]
                if n > 0:
                    pe.wait_ge(lo_done, g + 1)
                if n >= 2:
                    pe.wait_ge(proj_out, n - 1)
                w = [t[:, g % 2, :].rearrange("p (k c) -> p k c", k=KD) for t in (whi, wlo)]
                kind = tile_kind(n)
                if kind in ("T", "gate"):
                    for k in range(KD):
                        if n == 0:
                            if k % 2 == 0 and k < 6:
                                pe.wait_ge(first_lo, k // 2 + 1)
                            elif k == 6:
                                pe.wait_ge(lo_done, 1)
                            pe.wait_ge(x_split_lo, k + 1)
                        c = slice(half * P, half * P + P)
                        last = split(b[:, :], w[0][:, k, c], w[1][:, k, c], xhi[:, k, :], xlo[:, k, :], k == 0, k == KD - 1)
                else:
                    for c in range(2):
                        i = 2 * half + c
                        rows = slice(i * P, (i + 1) * P) if kind == "dv" or g == 6 else slice(i, S, 4)
                        for k in range(KD):
                            last = split(b[:, c * 256:(c + 1) * 256], xhi[:, k, rows], xlo[:, k, rows],
                                         w[0][:, k, :], w[1][:, k, :], k == 0, k == KD - 1)
                last.then_inc(proj_done, 1)

            for n in range(2 * N_DIL):
                proj(n)
            for s in range(SLOTS):
                n = tile_of_slot(s)
                if n is not None:
                    proj(n)
                if s == 0:
                    pe.wait_ge(proj_out, 2 * N_DIL)
                if s == DIFF0:
                    pe.wait_ge(proj_out, 2 * G_GATE)
                u = s
                if u < UNITS:
                    b0, b1 = bank[2], bank[3]
                    if u >= 1:
                        pe.wait_ge(logits_done, 2 * u)
                    if u < DIFF0:
                        r, h = dil(u)
                        for g in range(3):
                            f = (4 * g + h) // 2
                            rows = slice(HD * (h % 2), HD * (h % 2) + HD)
                            if g == 0:
                                mm(b0[:, :], lq[rows, f, r::4], lk[rows, f, :], start=True, stop=True)
                            else:
                                last = mm(b1[:, (g - 1) * P:g * P], lq[rows, f, r::4], lk[rows, f, r::4], start=True, stop=True)
                    else:
                        h, i = diff(u)
                        nk = P * (i + 1)
                        for c, b in ((0, b0), (1, b1)):
                            rows = slice(HD * c, HD * c + HD)
                            last = mm(b[:, 0:nk], dq[rows, h, i * P:(i + 1) * P], dk[rows, h, 0:nk], start=True, stop=True)
                    last.then_inc(scores_done, 1)
                yt = yt_of_slot(s)
                if yt:
                    r, j = yt
                    pe.wait_ge(y_done, 4 * r + 4)
                    if 2 * r + j:
                        pe.wait_ge(yt_lo, 2 * r + j)
                    nc.tensor.transpose(bank[5][:, 0:P], yl[:, r % 2, j * P:(j + 1) * P], ident[:, :]).then_inc(yt_done, 1)
                u = s - 2
                if 0 <= u < UNITS:
                    pe.wait_ge(pT_a, u + 1)
                    if u >= 1:
                        pe.wait_ge(y_done, u)
                    if u < DIFF0:
                        pe.wait_ge(pT_b, u + 1)
                        r, h = dil(u)
                        vals = [lv[:, 0, b, h * HD:(h + 1) * HD] for b in range(4)] + \
                               [lv[:, g, r, h * HD:(h + 1) * HD] for g in (1, 2)]
                        o = bank[4][:, 0:HD]
                    else:
                        h, i = diff(u)
                        vals = [dv[:, b, h * P:(h + 1) * P] for b in range(i + 1)]
                        o = bank[4][:, 0:P]
                    for b, v in enumerate(vals):
                        last = mm(o, pT[:, u % 2, b, :], v, start=b == 0, stop=b == len(vals) - 1)
                    last.then_inc(pv_done, 1)
                u = s - 1
                if 0 <= u < UNITS:
                    if u < DIFF0:
                        pe.wait_ge(probs_done, 2 * u + 2)
                        nb = 6
                    else:
                        pe.wait_ge(comb_done, u - DIFF0 + 1)
                        nb = diff(u)[1] + 1
                    if u >= 1:
                        pe.wait_ge(pT_a, u)
                        pe.wait_ge(pT_b, min(u, DIFF0))
                    for b in range(nb):
                        o = bank[6][:, b * P:(b + 1) * P] if b < 4 else bank[7][:, (b - 4) * P:(b - 3) * P]
                        last = nc.tensor.transpose(o, sc[:, u % 2, b * P:(b + 1) * P], ident[:, :])
                    last.then_inc(tr_done, 1)
            for n in LATE_GATES[:2]:
                proj(n)
            for h in range(HEADS):
                pe.wait_ge(norm_a, 1 + 4 * (h + 1))
                for i in range(TC):
                    last = nc.tensor.transpose(bank[2 + h][:, i * P:(i + 1) * P], yd[:, i, h * P:(h + 1) * P], ident[:, :])
                last.then_inc(yt_done, 1)
            for n in LATE_GATES[2:]:
                proj(n)
            pe.wait_ge(yt_lo, 8 + HEADS)
            pe.wait_ge(proj_out, 2 * G_BR)
            for m in range(KD):
                g = G_BR + m // 2
                pe.wait_ge(lo_done, g + 1)
                if m >= 2:
                    pe.wait_ge(prods_done, m - 1)
                w = [t[:, g % 2, 0:6 * 256].rearrange("p (k c) -> p k c", k=6) for t in (whi, wlo)]
                c = slice((m % 2) * P, (m % 2) * P + P)
                for b, hi, lo, k0, nk in ((0, yahi, yalo, 0, 4), (1, ybhi, yblo, 4, 2)):
                    for k in range(nk):
                        last = split(bank[2 * (m % 2) + b][:, :], w[0][:, k0 + k, c], w[1][:, k0 + k, c],
                                     hi[:, k, :], lo[:, k, :], k == 0, k == nk - 1)
                last.then_inc(za_done, 1)
            pe.wait_ge(prods_done, KD)
            def out_block(gi, c, j):
                rows, sl = slice(c * P, (c + 1) * P), (G_WO + gi) % 2
                for k in range(2):
                    cols = slice(k * D + j * S, k * D + (j + 1) * S)
                    last = split(bank[2 * c + j][:, :], xhi[:, 2 * gi + k, rows], xlo[:, 2 * gi + k, rows],
                                 whi[:, sl, cols], wlo[:, sl, cols], gi == 0 and k == 0, gi == N_WO - 1 and k == 1)
                return last

            for gi in range(N_WO - 2):
                pe.wait_ge(lo_done, G_WO + gi + 1)
                pe.wait_ge(mix_lo, 2 * gi + 2)
                for c in range(TC):
                    for j in range(2):
                        last = out_block(gi, c, j)
                last.then_inc(wo_group, 1)
            pe.wait_ge(lo_done, G_WQ - 1)
            pe.wait_ge(mix_lo, KD)
            for c, gi in ((0, 2), (1, 2), (0, 3), (1, 3), (2, 2), (2, 3), (3, 2), (3, 3)):
                if (c, gi) == (0, 3):
                    pe.wait_ge(lo_done, G_WQ)
                for j in range(2):
                    last = out_block(gi, c, j)
                if gi == 3:
                    last.then_inc(wo_done, 1)
            for c in range(TC):
                pe.wait_ge(ln_out, c + 1)
                for j in range(2):
                    for k in range(4):
                        last = nc.tensor.transpose(bank[2 * c + j][:, k * P:(k + 1) * P],
                                                   xn[:, c, (4 * j + k) * P:(4 * j + k + 1) * P], ident[:, :])
                    last.then_inc(xt_done, 1)

            def key_scores(n):
                pe.wait_ge(q_out, n + 1)
                if n >= 4:
                    pe.wait_ge(s_used, n - 3)
                for c in range(TC):
                    last = mm(bank[4 + n % 4][:, c * P:(c + 1) * P], qT[:, n % 2, c * P:(c + 1) * P], keys[:, n, :], start=True, stop=True)
                last.then_inc(s_done, 1)

            pe.wait_ge(xt_lo, 2 * TC)
            pe.wait_ge(keys_in, 32)
            for n in range(16):
                g = G_WQ + n // 2
                pe.wait_ge(lo_done, g + 1)
                if n >= 2:
                    pe.wait_ge(q_out, n - 1)
                w = [t[:, g % 2, :].rearrange("p (k c) -> p k c", k=KD) for t in (whi, wlo)]
                c = slice((n % 2) * P, (n % 2) * P + P)
                for k in range(KD):
                    last = split(bank[n % 2][:, :], w[0][:, k, c], w[1][:, k, c], xhi[:, k, :], xlo[:, k, :], k == 0, k == KD - 1)
                last.then_inc(q_done, 1)
                if n >= 1:
                    key_scores(n - 1)
            key_scores(15)

            def u_iteration(it, first=False, between=None):
                for s in range(2):
                    pe.wait_ge(lo_done, 2 * it + (G_U + s + 1))
                    sl = (G_U + s) % 2
                    w = [t[:, sl, :].rearrange("p (n k e) -> p n k e", n=2, k=KD) for t in (whi, wlo)]
                    for n in range(2):
                        t = 2 * s + n
                        if not first:
                            pe.wait_ge(h_gelu, 4 * it + (t - 3))
                        for k in range(KD):
                            last = split(bank[t][:, :], w[0][:, n, k, :], w[1][:, n, k, :], xhi[:, k, :], xlo[:, k, :], k == 0, k == KD - 1)
                        last.then_inc(h_done, 1)
                        if between is not None:
                            between(t)

            def transpose_picks(n):
                for c in range(TC):
                    last = nc.tensor.transpose(bank[4 + n][:, c * P:(c + 1) * P], picks[:, n, c, :], ident[:, :])
                last.then_inc(pt_done, 1)

            pe.wait_ge(q_out, 16)
            u_iteration(0, first=True)
            with pe.Fori(1, IT_A) as it:
                u_iteration(it)

            def picks_between(t):
                if t == 1:
                    pe.wait_ge(sel_done, TC)
                    transpose_picks(0)
                    transpose_picks(1)
                if t == 3:
                    pe.wait_ge(w_done, 1)
                    transpose_picks(2)

            u_iteration(IT_A, between=picks_between)
            pe.wait_ge(pt_out, 3)

            def build_set(n):
                for k in range(IT_S):
                    def tokens(t, k=k):
                        for q in quads_after(4 * k + t):
                            pe.wait_ge(g_free, n * QUADS + (q + 1))
                            pe.wait_ge(e_done, n * QUADS + (q + 1))
                            for i in range(4):
                                e, o = 4 * (q % 2) + i, g_bank(q, i // 2)[:, (i % 2) * 2 * P:(i % 2 + 1) * 2 * P]
                                last = mm(o, e2[:, e, :], e1[:, e, :, :].rearrange("p a k -> p (a k)"), start=True, stop=True)
                            last.then_inc(g_done, 1)
                    u_iteration(n * IT_S + (IT_0 + k), between=tokens)

            build_set(0)
            with pe.Fori(1, SETS) as n:
                build_set(n)
            u_iteration(N_U // 2 - 1)

            pe.wait_ge(g_free, S // 4 + 2)

            def v_block(t, c, j, first, last):
                rows = slice(c * P, (c + 1) * P)
                cols = slice((t % 2) * D + j * S, (t % 2) * D + (j + 1) * S)
                sl = (G_V + t // 2) % 2
                return split(bank[2 * c + j][:, :], ahi[:, t, rows], alo[:, t, rows],
                             whi[:, sl, cols], wlo[:, sl, cols], first, last)

            def v_iteration(it, first=False):
                for t in range(4):
                    if t % 2 == 0:
                        pe.wait_ge(lo_done, 2 * it + (G_V + t // 2 + 1))
                    pe.wait_ge(a_lo, 4 * it + (t + 1))
                    for c in range(TC):
                        for j in range(2):
                            if first and t == 0 and 2 * c + j < 4:
                                pe.wait_ge(h_gelu, NT - 3 + 2 * c + j)
                            last = v_block(t, c, j, first and t == 0, False)
                    last.then_inc(v_done, 1)

            v_iteration(0, first=True)
            with pe.Fori(1, N_U // 2 - 1) as it:
                v_iteration(it)
            pe.wait_ge(lo_done, G_V + N_U - 1)
            pe.wait_ge(a_lo, NT - 2)
            for c, g in ((0, 0), (1, 0), (2, 0), (0, 1), (1, 1), (2, 1), (3, 0), (3, 1)):
                if (c, g) == (0, 1):
                    pe.wait_ge(lo_done, G_V + N_U)
                    pe.wait_ge(a_lo, NT)
                for t in (2 * g, 2 * g + 1):
                    for j in range(2):
                        last = v_block(t, c, j, False, t == 3)
                if g == 1:
                    last.then_inc(ffn_done, 1)


def bucket(dist):
    n = np.maximum(dist, 0)
    nf = np.maximum(n, 1).astype(np.float32)
    large = 16 + (np.log(nf / np.float32(16)) / np.float32(math.log(2048 / 16)) * np.float32(16)).astype(np.int32)
    return np.where(n < 16, n, np.minimum(large, 31))


def bias_tiles(rel_bias):
    p = np.arange(P)[:, None]
    padded = np.concatenate([rel_bias, np.full((1, rel_bias.shape[1]), PAD, rel_bias.dtype)])

    def tile(dist, ok, heads):
        rows = np.where(ok, bucket(dist), rel_bias.shape[0])
        return np.ascontiguousarray(padded[rows][:, :, heads].transpose(0, 2, 1))

    d = p + (S - P) - np.arange(S)[None, :]
    diff = tile(d, d >= 0, slice(0, 4))
    d0 = 4 * p - (np.arange(S + 3)[None, :] - 3)
    d1 = 4 * (p - np.arange(P)[None, :])
    dil = [tile(d0, (d0 >= 0) & (d0 <= 128), slice(4, 8)), tile(d1, d1 >= 0, slice(8, 12)),
           tile(d1, (d1 >= 0) & (d1 % 16 == 0), slice(12, 16))]
    return diff, np.ascontiguousarray(np.concatenate(dil, axis=2))


def kernel(**inputs):
    import concourse.bacc as bacc
    from concourse.bass_utils import run_bass_kernel_spmd as run

    x = {k: np.asarray(v) for k, v in inputs.items()}

    def groups(w):
        n = w.shape[1] // 256
        return w.reshape(KD, P, n, 256).transpose(2, 1, 0, 3).reshape(n, P, GC)

    w_in = x["w_in"][0]
    ndq, nl = 3 * 512, 3 * 768
    w_in = np.concatenate([w_in[:, ndq:ndq + nl], w_in[:, :ndq], w_in[:, ndq + nl:]], axis=1)
    w_br = np.concatenate([x["w_branch_diff"][0], x["w_branch_dil"][0]])
    bias_d, bias_l = bias_tiles(x["rel_bias"])
    cst = np.array([STARTS[1:], np.diff(STARTS), np.arange(1, TOPK)], np.float32)
    arrays = {
        "x_t": x["x"][0].T.reshape(KD, P, S).transpose(1, 0, 2).reshape(P, KD * S),
        "x_n": x["x"][0].reshape(TC, P, D).transpose(1, 0, 2),
        "w_in": groups(w_in),
        "w_br": w_br.reshape(6, P, N_BR, 256).transpose(2, 1, 0, 3).reshape(N_BR, P, 6 * 256),
        "w_out": x["w_out"][0].reshape(KD, P, D).transpose(1, 0, 2),
        "w_q": groups(x["peer_wq"][0]),
        "keys": x["peer_keys"][0].reshape(16, P, P).transpose(2, 0, 1),
        "u": x["peer_u"][0].reshape(N_U, 2, P, KD, P).transpose(0, 4, 1, 3, 2).reshape(N_U, P, GC),
        "v": x["peer_v"][0].reshape(N_U, 2, P, D).transpose(0, 2, 1, 3).reshape(N_U, P, GC),
        "bias_d": bias_d, "bias_l": bias_l, "cst": cst,
        "diff_lambda": x["diff_lambda"].reshape(-1), "subln_g": x["diff_subln_g"].reshape(-1),
        "ln1_g": x["ln1_g"].reshape(-1), "ln1_b": x["ln1_b"].reshape(-1),
        "ln2_g": x["ln2_g"].reshape(-1), "ln2_b": x["ln2_b"].reshape(-1),
    }
    arrays = {k: np.ascontiguousarray(v) for k, v in arrays.items()}
    nc = bacc.Bacc("TRN2", target_bir_lowering=False, num_devices=1)
    aps = {k: nc.dram_tensor("in_" + k, v.shape, F32, kind="ExternalInput").ap() for k, v in arrays.items()}
    aps["out"] = nc.dram_tensor("out", [P, TC, D], F32, kind="ExternalOutput").ap()
    program(nc, aps)
    r = run(nc, [{"in_" + k: v for k, v in arrays.items()}], core_ids=[0])
    return r.results[0]["out"].transpose(1, 0, 2).reshape(1, S, D)
```
